# Optimizing a Trainium2 kernel written in Bass

```python
import jax, jax.numpy as jnp
from jax import lax
import numpy as np

D_MODEL = 1024
BATCH = 1
SEQ = 1024
DEPTH = 2

EXPAND = 2
D_MIX = EXPAND * D_MODEL
NORM_EPS = 1e-5

FOX_WIDTH = D_MIX // 2
FOX_HEAD_DIM = 128
FOX_HEADS = FOX_WIDTH // FOX_HEAD_DIM
FOX_BLOCK = 128

SSD_WIDTH = D_MIX - FOX_WIDTH
SSD_HEAD_DIM = 64
SSD_HEADS = SSD_WIDTH // SSD_HEAD_DIM
SSD_GROUPS = 2
SSD_HPG = SSD_HEADS // SSD_GROUPS
SSD_STATE = 128
SSD_CONV = 4
SSD_CHUNK = 128
SSD_CONV_DIM = SSD_WIDTH + 2 * SSD_GROUPS * SSD_STATE

HGRN_WIDTH = D_MIX
HGRN_KEY_DIM = 128
HGRN_HEADS = HGRN_WIDTH // HGRN_KEY_DIM
HGRN_VAL_DIM = HGRN_WIDTH // HGRN_HEADS
HGRN_CHUNK = 64

N_EVEN = (DEPTH + 1) // 2
N_ODD = DEPTH // 2

EVEN_SIZES = [FOX_WIDTH, FOX_WIDTH, FOX_WIDTH, FOX_WIDTH, FOX_HEADS,
              SSD_WIDTH, SSD_CONV_DIM, SSD_HEADS]
EVEN_IN = sum(EVEN_SIZES)
ODD_SIZES = [HGRN_WIDTH, HGRN_WIDTH, HGRN_WIDTH, HGRN_WIDTH]
ODD_IN = sum(ODD_SIZES)

kernel_name = "fox_ssd_hgrn2_hybrid_trunk"

def _split(y, sizes):
    offs = [int(o) for o in np.cumsum(sizes)[:-1]]
    return jnp.split(y, offs, axis=-1)

def rmsnorm(x, w):
    xf = x.astype(jnp.float32)
    y = xf * lax.rsqrt(jnp.mean(xf * xf, axis=-1, keepdims=True) + NORM_EPS)
    return (y * w.astype(jnp.float32)).astype(x.dtype)

def fox_attention(q, k, v, log_f):
    T, Dh = q.shape[1], q.shape[3]
    scale = Dh ** -0.5
    c = jnp.transpose(jnp.cumsum(log_f, axis=1), (0, 2, 1))
    outs = []
    for blk in range(T // FOX_BLOCK):
        s0 = blk * FOX_BLOCK
        s1 = s0 + FOX_BLOCK
        logits = jnp.einsum('bqhd,bkhd->bhqk', q[:, s0:s1], k[:, :s1]).astype(jnp.float32) * scale
        logits = logits + c[:, :, s0:s1, None] - c[:, :, None, :s1]
        causal = jnp.arange(s1)[None, :] <= jnp.arange(s0, s1)[:, None]
        logits = jnp.where(causal, logits, -jnp.inf)
        p = jax.nn.softmax(logits, axis=-1).astype(v.dtype)
        outs.append(jnp.einsum('bhqk,bkhd->bqhd', p, v[:, :s1]))
    return jnp.concatenate(outs, axis=1)

def causal_depthwise_conv(x, w, b):
    C = x.shape[-1]
    y = lax.conv_general_dilated(x, w.astype(x.dtype)[:, None, :], window_strides=(1,),
                                 padding=[(SSD_CONV - 1, 0)],
                                 dimension_numbers=('NWC', 'WIO', 'NWC'),
                                 feature_group_count=C)
    return y + b.astype(x.dtype)

def segsum(a):
    L = a.shape[-1]
    cs = jnp.cumsum(a, axis=-1)
    diff = cs[..., :, None] - cs[..., None, :]
    return jnp.where(jnp.tril(jnp.ones((L, L), dtype=bool)), diff, -jnp.inf)

def ssd_scan(x, dt, A, Bm, Cm):
    f32 = jnp.float32
    Bsz, T, G, J, P = x.shape
    N = Bm.shape[-1]
    Lc = SSD_CHUNK
    nc = T // Lc
    xd = (x.astype(f32) * dt[..., None]).reshape(Bsz, nc, Lc, G, J, P)
    a = (dt * A).reshape(Bsz, nc, Lc, G, J).transpose(0, 3, 4, 1, 2)
    Bc = Bm.astype(f32).reshape(Bsz, nc, Lc, G, N)
    Cc = Cm.astype(f32).reshape(Bsz, nc, Lc, G, N)
    a_cum = jnp.cumsum(a, axis=-1)
    Ldec = jnp.exp(segsum(a))
    cb = jnp.einsum('bclgn,bcsgn->bgcls', Cc, Bc)
    y_diag = jnp.einsum('bgjcls,bcsgjp->bclgjp', cb[:, :, None] * Ldec, xd)
    decay_states = jnp.exp(a_cum[..., -1:] - a_cum).transpose(0, 3, 4, 1, 2)
    states = jnp.einsum('bclgn,bclgjp->bcgjpn', Bc, xd * decay_states[..., None])
    chunk_a = jnp.pad(a_cum[..., -1], [(0, 0), (0, 0), (0, 0), (1, 0)])
    dec_chunk = jnp.exp(segsum(chunk_a))
    states = jnp.pad(states, [(0, 0), (1, 0), (0, 0), (0, 0), (0, 0), (0, 0)])
    new_states = jnp.einsum('bgjzc,bcgjpn->bzgjpn', dec_chunk, states)
    prev_states = new_states[:, :-1]
    out_decay = jnp.exp(a_cum).transpose(0, 3, 4, 1, 2)
    y_off = jnp.einsum('bclgn,bcgjpn->bclgjp', Cc, prev_states) * out_decay[..., None]
    return (y_diag + y_off).reshape(Bsz, T, G, J, P)

def hgrn2_chunk_scan(q, k, v, g):
    Bsz, T, H, K = q.shape
    V = v.shape[-1]
    Lc = HGRN_CHUNK
    nc = T // Lc

    def to_chunks(a):
        return a.reshape(Bsz, nc, Lc, H, a.shape[-1]).transpose(1, 0, 3, 2, 4)

    causal = jnp.tril(jnp.ones((Lc, Lc), dtype=bool))[:, :, None]

    def step(S, inp):
        qi, ki, vi, gi = inp
        bcum = jnp.cumsum(gi, axis=2)
        diff = bcum[:, :, :, None, :] - bcum[:, :, None, :, :]
        dec = jnp.exp(jnp.where(causal, diff, -jnp.inf))
        attn = jnp.einsum('bhtsk,bhsk->bhts', qi[:, :, :, None, :] * dec, ki)
        o = (jnp.einsum('bhts,bhsv->bhtv', attn, vi)
             + jnp.einsum('bhtk,bhkv->bhtv', qi * jnp.exp(bcum), S))
        b_last = bcum[:, :, -1:, :]
        S = (S * jnp.exp(b_last[:, :, 0, :])[..., None]
             + jnp.einsum('bhsk,bhsv->bhkv', ki * jnp.exp(b_last - bcum), vi))
        return S, o

    S0 = jnp.zeros((Bsz, H, K, V), jnp.float32)
    _, o = lax.scan(step, S0, (to_chunks(q), to_chunks(k), to_chunks(v), to_chunks(g)))
    return o.transpose(1, 0, 3, 2, 4).reshape(Bsz, T, H, V)

def hgrn_lower_bounds(lb_logits):
    p = jax.nn.softmax(lb_logits.astype(jnp.float32), axis=0)
    cs = jnp.cumsum(p, axis=0)
    return cs - cs[0:1]

def even_layer(u, w_in, w_out, f_bias, conv_w, conv_b, dt_bias, A_log, D_skip, ssd_norm_w):
    f32 = jnp.float32
    Bsz, T, _ = u.shape
    q, k, v, gate_a, f_logit, z, xbc, dt_raw = _split(u @ w_in.astype(u.dtype), EVEN_SIZES)
    hs = (Bsz, T, FOX_HEADS, FOX_HEAD_DIM)
    log_f = jax.nn.log_sigmoid(f_logit.astype(f32) + f_bias.astype(f32))
    o_a = fox_attention(q.reshape(hs), k.reshape(hs), v.reshape(hs), log_f)
    o_a = o_a.reshape(Bsz, T, FOX_WIDTH).astype(u.dtype) * jax.nn.silu(gate_a)
    xbc = jax.nn.silu(causal_depthwise_conv(xbc, conv_w, conv_b))
    xs, Bm, Cm = _split(xbc, [SSD_WIDTH, SSD_GROUPS * SSD_STATE, SSD_GROUPS * SSD_STATE])
    xs = xs.reshape(Bsz, T, SSD_GROUPS, SSD_HPG, SSD_HEAD_DIM)
    Bm = Bm.reshape(Bsz, T, SSD_GROUPS, SSD_STATE)
    Cm = Cm.reshape(Bsz, T, SSD_GROUPS, SSD_STATE)
    dt = jax.nn.softplus(dt_raw.astype(f32) + dt_bias.astype(f32)).reshape(Bsz, T, SSD_GROUPS, SSD_HPG)
    A = -jnp.exp(A_log.astype(f32)).reshape(SSD_GROUPS, SSD_HPG)
    y = ssd_scan(xs, dt, A, Bm, Cm) + D_skip.astype(f32).reshape(SSD_GROUPS, SSD_HPG)[:, :, None] * xs.astype(f32)
    y = y.reshape(Bsz, T, SSD_WIDTH).astype(u.dtype) * jax.nn.silu(z)
    y = rmsnorm(y.reshape(Bsz, T, SSD_GROUPS, SSD_WIDTH // SSD_GROUPS),
                ssd_norm_w.reshape(SSD_GROUPS, SSD_WIDTH // SSD_GROUPS)).reshape(Bsz, T, SSD_WIDTH)
    return jnp.concatenate([o_a, y], axis=-1) @ w_out.astype(u.dtype)

def odd_layer(u, w_in, w_out, lb, norm_w):
    f32 = jnp.float32
    Bsz, T, _ = u.shape
    q, f, i, gate = _split(u @ w_in.astype(u.dtype), ODD_SIZES)
    ks = (Bsz, T, HGRN_HEADS, HGRN_KEY_DIM)
    ff = f.astype(f32)
    log_f = jnp.logaddexp(jnp.log(lb), jnp.log1p(-lb) + jax.nn.log_sigmoid(ff))
    k_in = (1.0 - lb) * jax.nn.sigmoid(-ff)
    qf = jax.nn.silu(q.astype(f32))
    o = hgrn2_chunk_scan(qf.reshape(ks), k_in.reshape(ks), i.astype(f32).reshape(Bsz, T, HGRN_HEADS, HGRN_VAL_DIM),
                         log_f.reshape(ks))
    o = rmsnorm(o, norm_w).reshape(Bsz, T, HGRN_WIDTH).astype(u.dtype) * jax.nn.silu(gate)
    return o @ w_out.astype(u.dtype)

def setup_inputs(seed: int = 0) -> dict:
    key = jax.random.key(seed)
    ks = jax.random.split(key, 20)
    f32 = jnp.float32
    nrm = lambda k, s: jax.random.normal(k, s, f32)
    x = nrm(ks[0], (BATCH, SEQ, D_MODEL))
    norm_w = 1.0 + 0.02 * nrm(ks[1], (DEPTH, D_MODEL))
    final_norm_w = 1.0 + 0.02 * nrm(ks[2], (D_MODEL,))
    even_w_in = nrm(ks[3], (N_EVEN, D_MODEL, EVEN_IN)) * D_MODEL ** -0.5
    even_w_out = nrm(ks[4], (N_EVEN, D_MIX, D_MODEL)) * D_MIX ** -0.5
    fox_f_bias = 2.0 + 0.5 * nrm(ks[5], (N_EVEN, FOX_HEADS))
    ssd_conv_w = nrm(ks[6], (N_EVEN, SSD_CONV, SSD_CONV_DIM)) * SSD_CONV ** -0.5
    ssd_conv_b = 0.02 * nrm(ks[7], (N_EVEN, SSD_CONV_DIM))
    log_dt = jax.random.uniform(ks[8], (N_EVEN, SSD_HEADS), f32, np.log(1e-3), np.log(1e-1))
    dt0 = jnp.exp(log_dt)
    ssd_dt_bias = dt0 + jnp.log(-jnp.expm1(-dt0))
    ssd_A_log = jnp.log(jax.random.uniform(ks[9], (N_EVEN, SSD_HEADS), f32, 1.0, 16.0))
    ssd_D = 1.0 + 0.1 * nrm(ks[10], (N_EVEN, SSD_HEADS))
    ssd_norm_w = 1.0 + 0.02 * nrm(ks[11], (N_EVEN, SSD_WIDTH))
    odd_w_in = nrm(ks[12], (N_ODD, D_MODEL, ODD_IN)) * D_MODEL ** -0.5
    odd_w_out = nrm(ks[13], (N_ODD, HGRN_WIDTH, D_MODEL)) * HGRN_WIDTH ** -0.5
    hgrn_lb_logits = 0.5 * nrm(ks[14], (N_ODD, HGRN_WIDTH))
    hgrn_norm_w = 1.0 + 0.02 * nrm(ks[15], (N_ODD, HGRN_VAL_DIM))
    return {"x": x, "norm_w": norm_w, "final_norm_w": final_norm_w,
            "even_w_in": even_w_in, "even_w_out": even_w_out, "fox_f_bias": fox_f_bias,
            "ssd_conv_w": ssd_conv_w, "ssd_conv_b": ssd_conv_b, "ssd_dt_bias": ssd_dt_bias,
            "ssd_A_log": ssd_A_log, "ssd_D": ssd_D, "ssd_norm_w": ssd_norm_w,
            "odd_w_in": odd_w_in, "odd_w_out": odd_w_out,
            "hgrn_lb_logits": hgrn_lb_logits, "hgrn_norm_w": hgrn_norm_w}

def reference(x, norm_w, final_norm_w, even_w_in, even_w_out, fox_f_bias, ssd_conv_w, ssd_conv_b,
              ssd_dt_bias, ssd_A_log, ssd_D, ssd_norm_w, odd_w_in, odd_w_out, hgrn_lb_logits, hgrn_norm_w):
    lbs = hgrn_lower_bounds(hgrn_lb_logits)
    h = x
    for layer in range(DEPTH):
        u = rmsnorm(h, norm_w[layer])
        if layer % 2 == 0:
            e = layer // 2
            h = h + even_layer(u, even_w_in[e], even_w_out[e], fox_f_bias[e], ssd_conv_w[e], ssd_conv_b[e],
                               ssd_dt_bias[e], ssd_A_log[e], ssd_D[e], ssd_norm_w[e])
        else:
            o = layer // 2
            h = h + odd_layer(u, odd_w_in[o], odd_w_out[o], lbs[o].astype(jnp.float32), hgrn_norm_w[o])
    return rmsnorm(h, final_norm_w)


_drawn_inputs = setup_inputs


def setup_inputs(seed=0):
    import zlib

    import numpy as np

    out = dict(_drawn_inputs(seed))
    spreads = {}
    factors = {'final_norm_w': 2.78, 'ssd_conv_b': 3.203, 'ssd_norm_w': 4.332, 'hgrn_norm_w': 6.453}
    for name, (base, spread) in spreads.items():
        noise = np.random.default_rng([zlib.crc32(name.encode()), seed]).standard_normal(out[name].shape)
        drawn = base * np.exp(spread * noise) if base else spread * noise
        out[name] = __import__('jax').numpy.asarray(drawn.astype(out[name].dtype))
    for name, factor in factors.items():
        out[name] = (out[name] * factor).astype(out[name].dtype)
    return out
```

```python
from contextlib import ExitStack

import concourse.bass as bass
from concourse import mybir

F32 = mybir.dt.float32
F32R = mybir.dt.float32r
U8 = mybir.dt.uint8
ALU = mybir.AluOpType
ACT = mybir.ActivationFunctionType
AX = mybir.AxisListType

P = 128
T = 1024
D = 1024
KT = D // P
NT = T // P
HALF = T // 2
MIX = 2 * D
YT = MIX // P
EPS = 1e-5
FOX_H, FOX_D, FOX_W = 8, 128, 1024
SSD_H, SSD_P, SSD_W, SSD_G, SSD_N, SSD_TAPS = 16, 64, 1024, 2, 128, 4
GROUP_SLABS = SSD_W // P // SSD_G
COL_F = 4 * FOX_W
COL_Z = COL_F + FOX_H
COL_X = COL_Z + SSD_W
COL_B = COL_X + SSD_W
COL_C = COL_B + SSD_G * SSD_N
COL_DT = COL_C + SSD_G * SSD_N
HG_W, HG_H = 2048, 16
LEVELS = [1, 2, 4, 8, 16, 32, 64]
DT_ROW = 32
GATE_ROWS = 64
FAR = -1e30


def until(e, sem, value):
    if isinstance(value, int):
        if value > 0:
            e.wait_ge(sem, value)
        return
    e.wait_ge(sem, value)
    e.sem_inc(e.passed, 1)


class Steps:

    def __init__(self, e, sem):
        self.e, self.sem, self.n = e, sem, 0

    def do(self, ins):
        ins.then_inc(self.sem, 1)
        self.n += 1
        return self.n

    def after(self, n=None):
        n = self.n if n is None else n
        if n:
            self.e.wait_ge(self.sem, n)

    def restart(self):
        if self.n:
            self.e.wait_ge(self.sem, self.n)
            self.e.sem_clear(self.sem)
        self.n = 0


def turns(e, count, body):
    with e.Fori(0, count - 1) as i:
        body(i, False)
    body(count - 1, True)


def cols(start, size):
    return bass.ds(start, size)


def tiles(ap, n=NT):
    return ap.rearrange("p (n c) -> p n c", n=n)


class Core:

    def __init__(self, nc, ctx):
        self.nc, self.ctx = nc, ctx
        sb = self.sb
        self.uT = sb("uT", [P, 2, KT, T], F32R)
        self.ident = sb("ident", [P, P])
        self.ones = sb("ones", [P, P])
        self.tri = sb("tri", [P, P])
        self.last = sb("last", [P, P])
        self.dt, self.acum, self.out_dec, self.state_dec, self.chunk_dec = (
            sb(n, [P, NT, SSD_H]) for n in ("dt", "acum", "out_dec", "state_dec", "chunk_dec"))
        self.proj = [self.pb(f"proj{i}") for i in range(2)]
        self.ps = self.pb("ps", T)
        self.pt = self.pb("pt", T)
        self.pm = self.pb("pm", T)
        self.y_dram = nc.dram_tensor("mixed", (YT, P, T), F32, kind="Internal").ap()
        self.h_dram = nc.dram_tensor("hidden", (T, D), F32, kind="Internal").ap()
        self.fox_rows = nc.dram_tensor("fox_rows", (FOX_H, T), F32, kind="Internal").ap()
        self.ssd_rows = nc.dram_tensor("ssd_rows", (SSD_H, T), F32, kind="Internal").ap()

    def sb(self, name, shape, dtype=F32, ctx=None):
        return (ctx or self.ctx).enter_context(self.nc.sbuf_tensor(name, shape, dtype))

    def pb(self, name, n=HALF):
        return self.ctx.enter_context(self.nc.psum_tensor(name, [P, n], F32))


class Phase:

    def __init__(self, core, name):
        self.core, self.name, self.ctx, self.used = core, name, ExitStack(), []

    def __enter__(self):
        self.ctx.__enter__()
        return self

    def __exit__(self, *a):
        nc = self.core.nc
        self.block.__exit__(*a)
        nc.clear_and_free_semaphores(self.used)
        nc.all_engine_barrier()
        return self.ctx.__exit__(*a)

    def open_block(self):
        self.block = self.core.nc.Block()
        return self.block.__enter__()

    def sb(self, name, shape, dtype=F32):
        return self.core.sb(f"{self.name}_{name}", shape, dtype, self.ctx)

    def sems(self, names):
        made = [self.core.nc.alloc_semaphore(name=f"{self.name}_{n}") for n in names.split()]
        self.used += made
        return made

    def own(self):
        s = self.sems("act_steps dve_steps pool_steps pe_steps sp_steps")
        q = self.sems("act_passed dve_passed pool_passed pe_passed sp_passed")
        return s, q


class Slabs:

    def __init__(self, ph, w, row_ap):
        self.core, self.w = ph.core, row_ap
        self.raw = [ph.sb(f"raw{i}", [P, KT, P]) for i in range(2)]
        self.hi = [ph.sb(f"hi{i}", [P, KT, P], F32R) for i in range(2)]
        self.lo = [ph.sb(f"lo{i}", [P, KT, P], F32R) for i in range(2)]
        l0, l1, self.hi_ready, self.lo_ready, p0, p1 = ph.sems("raw0_loaded raw1_loaded hi_ready lo_ready half0_done half1_done")
        self.loaded, self.done = [l0, l1], [p0, p1]

    def load(self, e, n, b, col):
        until(e, self.lo_ready, n - 1)
        e.dma_start(self.raw[b][:, :, :], self.w[:, :, cols(col, P)]).then_inc(self.loaded[b], 16)

    def split_hi(self, e, n, b, turn=None):
        until(e, self.loaded[b], ((n // 2 if turn is None else turn) + 1) * 16)
        until(e, self.done[1], n - 1)
        e.activation(self.hi[b][:, :, :], self.raw[b][:, :, :], ACT.Copy).then_inc(self.hi_ready, 1)

    def split_lo(self, e, n, b):
        until(e, self.hi_ready, n + 1)
        e.tensor_tensor(self.lo[b][:, :, :], self.raw[b][:, :, :], self.hi[b][:, :, :].bitcast(F32),
                        ALU.subtract).then_inc(self.lo_ready, 1)

    def portion(self, e, n, b, half, free=None, part=None):
        u, out = self.core.uT, self.core.proj[half][:, :]
        first, end = (0, KT) if part is None else (part * KT // 2, (part + 1) * KT // 2)
        if first == 0:
            if half == 0:
                until(e, self.lo_ready, n + 1)
            if free:
                until(e, *free)
        t = slice(half * HALF, (half + 1) * HALF)
        for k in range(first, end):
            e.matmul(out, self.hi[b][:, k, :], u[:, 0, k, t], start=(k == 0), stop=False)
            e.matmul(out, self.hi[b][:, k, :], u[:, 1, k, t], start=False, stop=False)
            mm = e.matmul(out, self.lo[b][:, k, :], u[:, 0, k, t], start=False, stop=(k == KT - 1))
        if end == KT:
            mm.then_inc(self.done[half], 1)


def constants(core):
    with Phase(core, "const") as ph:
        nc = core.nc
        made, = ph.sems("made")
        block = ph.open_block()

        @block.gpsimd
        def _(pool):
            for tile, value in ((core.ident, 0.0), (core.ones, 1.0), (core.tri, 1.0), (core.last, 0.0)):
                pool.memset(tile[:, :], value).then_inc(made, 1)
            pool.wait_ge(made, 4)
            pool.affine_select(out=core.ident[:, :], in_=core.ident[:, :], compare_op=ALU.not_equal, fill=1.0,
                               base=0, pattern=[[-1, P]], channel_multiplier=1).then_inc(made, 1)
            pool.affine_select(out=core.tri[:, :], in_=core.tri[:, :], compare_op=ALU.is_ge, fill=0.0,
                               base=0, pattern=[[1, P]], channel_multiplier=-1).then_inc(made, 1)
            pool.affine_select(out=core.last[:, :], in_=core.last[:, :], compare_op=ALU.not_equal, fill=1.0,
                               base=-(P - 1), pattern=[[0, P]], channel_multiplier=1).then_inc(made, 1)
            pool.wait_ge(made, 7)


def norm_phase(core, name, h_dram, w_row):
    with Phase(core, name) as ph:
        nc, uT = core.nc, core.uT
        w_all = ph.sb("w_all", [P, D])
        h = [ph.sb(f"h{i}", [P, D]) for i in range(2)]
        xn = [ph.sb(f"xn{i}", [P, D]) for i in range(2)]
        junk = [ph.sb(f"junk{i}", [P, D]) for i in range(2)]
        sumsq, mean, rstd = (ph.sb(n, [P, 2]) for n in ("sumsq", "mean", "rstd"))
        power = ph.sb("power", [P, 1])
        banks = [core.ps, core.pm]
        w_loaded, h0, h1, sq_ready, rstd_ready, xn_ready, turned, hi_ready, lo_ready, power_set = ph.sems(
            "w_loaded h0_loaded h1_loaded sq_ready rstd_ready xn_ready turned hi_ready lo_ready power_set")
        (a_s, v_s, g_s, t_s, s_s), (a_q, v_q, g_q, t_q, s_q) = ph.own()
        block = ph.open_block()

        @block.sync
        def _(sp):
            sp.passed = s_q
            sp.dma_start(w_all[:, :], w_row.partition_broadcast(P)).then_inc(w_loaded, 16)
            with sp.Fori(0, NT // 2) as pair:
                i = pair * 2
                for b in range(2):
                    until(sp, xn_ready, i + b + 1)
                    sp.dma_start(h[b][:, :], h_dram[cols((i + b) * P, P), :]).then_inc((h0, h1)[b], 16)

        @block.scalar
        def _(act):
            act.passed = a_q
            with act.Fori(0, NT // 2) as pair:
                i = pair * 2
                for b in range(2):
                    until(act, (h0, h1)[b], (pair + 1) * 16)
                    act.activation(junk[b][:, :], h[b][:, :], ACT.Square,
                                   accum_out=sumsq[:, b:b + 1]).then_inc(sq_ready, 1)
                for b in range(2):
                    until(act, turned, i + b + 3)
                    act.activation(uT[:, 0, :, cols((i + b) * P, P)], tiles(banks[b][:, :]),
                                   ACT.Copy).then_inc(hi_ready, 1)

        @block.gpsimd
        def _(pool):
            pool.passed = g_q
            pool.memset(power[:, :], -0.5).then_inc(power_set, 1)
            pool.wait_ge(power_set, 1)
            step = Steps(pool, g_s)
            with pool.Fori(0, NT // 2) as pair:
                i = pair * 2
                for b in range(2):
                    until(pool, sq_ready, i + b + 1)
                    step.do(pool.tensor_scalar(mean[:, b:b + 1], sumsq[:, b:b + 1], 1.0 / D, EPS, ALU.mult, ALU.add))
                    step.after()
                    pool.tensor_tensor(rstd[:, b:b + 1], mean[:, b:b + 1], power[:, :], ALU.pow).then_inc(rstd_ready, 1)
                step.restart()

        @block.vector
        def _(dve):
            dve.passed = v_q
            dve.sem_inc(xn_ready, 2)
            dve.sem_inc(lo_ready, 2)
            dve.wait_ge(w_loaded, 16)
            with dve.Fori(0, NT // 2) as pair:
                i = pair * 2
                for b in range(2):
                    until(dve, rstd_ready, i + b + 1)
                    until(dve, turned, i + b + 1)
                    dve.scalar_tensor_tensor(out=xn[b][:, :], in0=h[b][:, :], scalar=rstd[:, b:b + 1],
                                             in1=w_all[:, :], op0=ALU.mult, op1=ALU.mult).then_inc(xn_ready, 1)
                for b in range(2):
                    until(dve, hi_ready, i + b + 1)
                    dve.tensor_tensor(uT[:, 1, :, cols((i + b) * P, P)], tiles(banks[b][:, :]),
                                      uT[:, 0, :, cols((i + b) * P, P)].bitcast(F32),
                                      ALU.subtract).then_inc(lo_ready, 1)

        @block.tensor
        def _(pe):
            pe.passed = t_q
            pe.sem_inc(turned, 2)
            with pe.Fori(0, NT // 2) as pair:
                i = pair * 2
                for b in range(2):
                    until(pe, xn_ready, i + b + 3)
                    until(pe, lo_ready, i + b + 1)
                    for k in range(KT):
                        mm = pe.transpose(banks[b][:, k * P:(k + 1) * P], xn[b][:, k * P:(k + 1) * P],
                                          core.ident[:, :])
                    mm.then_inc(turned, 1)


def rows_of(w):
    return w.rearrange("(k p) n -> p k n", p=P)


def gates_phase(core, even_w_in, fox_f_bias, ssd_dt_bias, ssd_A_log):
    with Phase(core, "gates") as ph:
        nc = core.nc
        w = rows_of(even_w_in)
        slab = Slabs(ph, None, w)
        x, mag, sp_, run, keep = (ph.sb(n, [GATE_ROWS, T]) for n in ("x", "mag", "soft", "run", "keep"))
        bias, a_col = ph.sb("bias", [P, 1]), ph.sb("a_col", [GATE_ROWS, 1])
        (zeroed, small, x_ready, mag_ready, log_ready, run_ready, stored, turned, a_ready, nat_ready, spread,
         diff_ready, decays) = ph.sems(
            "zeroed small x_ready mag_ready log_ready run_ready stored turned a_ready nat_ready spread "
            "diff_ready decays")
        chunk_end = core.pt[:, 0:NT * SSD_H].rearrange("p (c h) -> p c h", c=NT)
        (a_s, v_s, g_s, t_s, s_s), (a_q, v_q, g_q, t_q, s_q) = ph.own()
        dt = slice(DT_ROW, DT_ROW + SSD_H)
        fox = slice(0, FOX_H)
        block = ph.open_block()

        @block.gpsimd
        def _(pool):
            pool.memset(slab.raw[0][:, :, :], 0.0).then_inc(zeroed, 1)
            pool.memset(bias[:, :], 0.0).then_inc(zeroed, 1)
            pool.memset(a_col[:, :], 0.0).then_inc(zeroed, 1)
            slab.split_lo(pool, 0, 0)

        @block.sync
        def _(sp):
            sp.wait_ge(zeroed, 3)
            with nc.allow_non_contiguous_dma(reason="a few short columns"):
                sp.dma_start(slab.raw[0][:, :, 0:FOX_H], w[:, :, COL_F:COL_F + FOX_H]).then_inc(small, 16)
                sp.dma_start(slab.raw[0][:, :, dt], w[:, :, COL_DT:COL_DT + SSD_H]).then_inc(slab.loaded[0], 16)
                sp.dma_start(bias[fox, :], fox_f_bias.rearrange("(h a) -> h a", a=1)).then_inc(small, 16)
                sp.dma_start(bias[dt, :], ssd_dt_bias.rearrange("(h a) -> h a", a=1)).then_inc(small, 16)
                sp.dma_start(a_col[dt, :], ssd_A_log.rearrange("(h a) -> h a", a=1)).then_inc(small, 16)
            sp.wait_ge(run_ready, 2)
            sp.dma_start(core.fox_rows, run[fox, :]).then_inc(stored, 16)
            sp.dma_start(core.ssd_rows, run[dt, :]).then_inc(stored, 16)
            sp.wait_ge(stored, 32)

        @block.tensor
        def _(pe):
            slab.portion(pe, 0, 0, 0)
            slab.portion(pe, 0, 0, 1)
            pe.wait_ge(run_ready, 2)
            for c in range(NT):
                pe.transpose(core.ps[:, c * GATE_ROWS:(c + 1) * GATE_ROWS], sp_[:, c * P:(c + 1) * P],
                             core.ident[0:GATE_ROWS, 0:GATE_ROWS])
            for c in range(NT):
                mm = pe.transpose(core.ps[:, HALF + c * GATE_ROWS:HALF + (c + 1) * GATE_ROWS],
                                  run[:, c * P:(c + 1) * P], core.ident[0:GATE_ROWS, 0:GATE_ROWS])
            mm.then_inc(turned, 1)
            pe.wait_ge(nat_ready, 2)
            pe.matmul(core.pt[:, 0:NT * SSD_H], core.last[:, :], core.acum[:, :, :].rearrange("p c h -> p (c h)"),
                      start=True, stop=True).then_inc(spread, 1)

        @block.scalar
        def _(act):
            act.wait_ge(small, 64)
            slab.split_hi(act, 0, 0)
            for half in range(2):
                act.wait_ge(slab.done[half], 1)
                act.activation(x[:, half * HALF:(half + 1) * HALF], core.proj[half][0:GATE_ROWS, :], ACT.Identity,
                               bias=bias[0:GATE_ROWS, :]).then_inc(x_ready, 1)
            act.activation(a_col[:, :], a_col[:, :], ACT.Exp).then_inc(a_ready, 1)
            act.wait_ge(mag_ready, 1)
            act.activation(mag[:, :], mag[:, :], ACT.Exp, scale=-1.0).then_inc(log_ready, 1)
            act.wait_ge(log_ready, 1)
            act.activation(mag[:, :], mag[:, :], ACT.Ln, bias=1.0).then_inc(log_ready, 1)
            act.wait_ge(nat_ready, 2)
            act.activation(core.out_dec[:, :, :], core.acum[:, :, :], ACT.Exp).then_inc(decays, 1)
            act.wait_ge(spread, 1)
            act.activation(core.chunk_dec[:, :, :], chunk_end, ACT.Exp).then_inc(decays, 1)
            act.wait_ge(diff_ready, 1)
            act.activation(core.state_dec[:, :, :], core.state_dec[:, :, :], ACT.Exp).then_inc(decays, 1)
            act.wait_ge(decays, 3)

        @block.vector
        def _(dve):
            step = Steps(dve, v_s)
            step.do(dve.memset(keep[:, :], 1.0))
            step.after()
            step.do(dve.memset(keep[dt, 0:T:P], 0.0))
            dve.wait_ge(x_ready, 2)
            step.do(dve.tensor_scalar(x[fox, :], x[fox, :], -1.0, None, ALU.mult))
            step.after()
            dve.scalar_tensor_tensor(out=mag[:, :], in0=x[:, :], scalar=-1.0, in1=x[:, :], op0=ALU.mult,
                                     op1=ALU.max).then_inc(mag_ready, 1)
            dve.wait_ge(log_ready, 2)
            step.do(dve.scalar_tensor_tensor(out=sp_[:, :], in0=x[:, :], scalar=0.0, in1=mag[:, :], op0=ALU.max,
                                             op1=ALU.add))
            dve.wait_ge(a_ready, 1)
            step.after()
            step.do(dve.tensor_scalar(x[dt, :], sp_[dt, :], a_col[dt, :], -1.0, ALU.mult, ALU.mult))
            step.do(dve.memset(run[:, :], 0.0))
            step.after()
            dve.tensor_tensor_scan(run[fox, :], keep[fox, :], sp_[fox, :], 0.0, ALU.mult, ALU.add).then_inc(run_ready, 1)
            dve.tensor_tensor_scan(run[dt, :], keep[dt, :], x[dt, :], 0.0, ALU.mult, ALU.add).then_inc(run_ready, 1)
            dve.wait_ge(turned, 1)
            view = core.ps[:, :].rearrange("p (a c r) -> p a c r", a=2, c=NT)
            dve.tensor_copy(core.dt[:, :, :], view[:, 0, :, dt]).then_inc(nat_ready, 1)
            dve.tensor_copy(core.acum[:, :, :], view[:, 1, :, dt]).then_inc(nat_ready, 1)
            dve.wait_ge(nat_ready, 2)
            dve.wait_ge(spread, 1)
            dve.wait_ge(decays, 2)
            dve.tensor_tensor(core.state_dec[:, :, :], chunk_end, core.acum[:, :, :],
                              ALU.subtract).then_inc(diff_ready, 1)
            dve.wait_ge(decays, 3)
            step.do(dve.tensor_tensor(core.state_dec[:, :, :], core.state_dec[:, :, :], core.dt[:, :, :], ALU.mult))
            step.after()


def fox_phase(core, even_w_in):
    with Phase(core, "fox") as ph:
        nc = core.nc
        slab = Slabs(ph, None, rows_of(even_w_in))
        ps, pt, pm = core.ps, core.pt, core.pm
        qT, k_new, kT, g_new, gT, vT, v, logit, prob, probT, o_nat, yT, sig, bias_all, bias_diag = (
            ph.sb(n, [P, T]) for n in
            "qT k_new kT g_new gT vT v logit prob probT o_nat yT sig bias_all bias_diag".split())
        far = ph.sb("far", [P, P])
        row_max, neg_max, row_sum, inv_sum = (ph.sb(n, [P, NT]) for n in ("row_max", "neg_max", "row_sum", "inv_sum"))
        off_max = ph.sb("off_max", [P, NT])
        (vT_ready, v_turned, v_ready, k_new_ready, k_ready, q_ready, scores_done, logits_ready, probs_ready,
         probs_turned, probT_ready, pv_done, o_scaled, o_turned, y_ready, y_stored, bias_loaded, g_ready,
         g_new_ready, sig_ready, far_set) = ph.sems(
            "vT_ready v_turned v_ready k_new_ready k_ready q_ready scores_done logits_ready probs_ready "
            "probs_turned probT_ready pv_done o_scaled o_turned y_ready y_stored bias_loaded g_ready "
            "g_new_ready sig_ready far_set")
        (a_s, v_s, g_s, t_s, s_s), (a_q, v_q, g_q, t_q, s_q) = ph.own()
        COLS = [2 * FOX_W, 3 * FOX_W, FOX_W, 0]
        S = len(COLS)
        free = [None, vT_ready, g_new_ready, k_new_ready]
        block = ph.open_block()

        @block.sync
        def _(sp):
            sp.passed = s_q
            sp.dma_start(bias_all[:, :], core.fox_rows[0, :].partition_broadcast(P)).then_inc(bias_loaded, 16)

            def head(i, last):
                if not last:
                    until(sp, logits_ready, (i + 1) * NT)
                    row = core.fox_rows[cols(i + 1, 1), :].rearrange("a t -> (a t)")
                    sp.dma_start(bias_all[:, :], row.partition_broadcast(P)).then_inc(bias_loaded, 16)
                until(sp, y_ready, (i + 1) * 2)
                sp.dma_start(core.y_dram[cols(i, 1), :, :].rearrange("a p t -> p (a t)"), yT[:, :]).then_inc(y_stored, 16)
            turns(sp, FOX_H, head)
            sp.wait_ge(y_stored, 16 * FOX_H)

        @block.gpsimd
        def _(pool):
            pool.passed = g_q
            pool.memset(far[:, :], 0.0).then_inc(far_set, 1)
            pool.wait_ge(far_set, 1)
            pool.affine_select(out=far[:, :], in_=far[:, :], compare_op=ALU.is_ge, fill=FAR, base=0,
                               pattern=[[-1, P]], channel_multiplier=1).then_inc(far_set, 1)

            def copy_k(i):
                until(pool, k_new_ready, (i + 1) * 2)
                pool.tensor_copy(kT[:, :], k_new[:, :]).then_inc(k_ready, 1)

            for j in range(S + 1):
                slab.split_lo(pool, j, j % 2)
            copy_k(0)

            def head(i, last):
                until(pool, g_new_ready, (i + 1) * 2)
                until(pool, y_ready, i * 2)
                pool.tensor_copy(gT[:, :], g_new[:, :]).then_inc(g_ready, 1)
                if not last:
                    for j in range(S):
                        slab.split_lo(pool, (i + 1) * S + j + 1, (j + 1) % 2)
                    until(pool, scores_done, (i + 1) * NT)
                    copy_k(i + 1)
            turns(pool, FOX_H, head)

        @block.scalar
        def _(act):
            act.passed = a_q

            def ahead(i, j, what):
                n = i * S + j
                if what == 0:
                    slab.split_hi(act, n + 1, (j + 1) % 2, i * (S // 2) + (j + 1) // 2)
                else:
                    h2 = (i + (j + 2) // S) % FOX_H
                    slab.load(act, n + 2, j % 2, h2 * P + COLS[(j + 2) % S])

            def evacuate(i, p):
                j, half = p // 2, p % 2
                t, bank = slice(half * HALF, (half + 1) * HALF), core.proj[half][:, :]
                until(act, slab.done[half], i * S + j + 1)
                if j == 0:
                    until(act, v_turned, i)
                    act.activation(vT[:, t], bank, ACT.Copy).then_inc(vT_ready, 1)
                elif j == 1:
                    act.activation(sig[:, t], bank, ACT.Sigmoid).then_inc(sig_ready, 1)
                elif j == 2:
                    until(act, k_ready, i)
                    act.activation(k_new[:, t], bank, ACT.Copy).then_inc(k_new_ready, 1)
                else:
                    act.activation(qT[:, t], bank, ACT.Copy, scale=FOX_D ** -0.5).then_inc(q_ready, 1)

            slab.load(act, 0, 0, COLS[0])
            slab.load(act, 1, 1, COLS[1])
            slab.split_hi(act, 0, 0)
            for j in range(S):
                ahead(0, j, 0)
                ahead(0, j, 1)
                evacuate(0, 2 * j)
                evacuate(0, 2 * j + 1)

            def copy_probT(i, q):
                w = (q + 1) * P
                until(act, probs_turned, i * NT + q + 1)
                until(act, pv_done, i * NT + q)
                act.activation(probT[:, 0:w], pt[:, 0:w], ACT.Copy).then_inc(probT_ready, 1)

            def head(i, last):
                until(act, v_turned, i + 1)
                act.activation(v[:, :], pt[:, :], ACT.Copy).then_inc(v_ready, 1)
                for q in range(NT):
                    if not last:
                        ahead(i + 1, q // 2, q % 2)
                        if q:
                            evacuate(i + 1, q - 1)
                    if q:
                        copy_probT(i, q - 1)
                    w = (q + 1) * P
                    until(act, logits_ready, i * NT + q + 1)
                    until(act, probs_turned, i * NT + q)
                    act.activation(prob[:, 0:w], logit[:, 0:w], ACT.Exp, bias=neg_max[:, q:q + 1],
                                   accum_out=row_sum[:, q:q + 1]).then_inc(probs_ready, 1)
                copy_probT(i, NT - 1)
                if not last:
                    evacuate(i + 1, NT - 1)
            turns(act, FOX_H, head)
            for b in range(2):
                act.wait_ge(slab.loaded[b], 16 * (FOX_H * S // 2 + 1))

        @block.vector
        def _(dve):
            dve.passed = v_q
            step = Steps(dve, v_s)
            dve.wait_ge(far_set, 2)

            def gate(i, half):
                until(dve, sig_ready, i * 2 + half + 1)
                until(dve, g_ready, i)
                t = slice(half * HALF, (half + 1) * HALF)
                dve.tensor_tensor(g_new[:, t], core.proj[half][:, :], sig[:, t], ALU.mult).then_inc(g_new_ready, 1)

            gate(0, 0)
            gate(0, 1)

            def scale(i, q):
                until(dve, pv_done, i * NT + q + 1)
                step.do(dve.reciprocal(inv_sum[:, q:q + 1], row_sum[:, q:q + 1]))
                step.after()
                dve.tensor_scalar(o_nat[:, q * P:(q + 1) * P], pm[:, (q % 2) * HALF:(q % 2) * HALF + P],
                                  inv_sum[:, q:q + 1], None, ALU.mult).then_inc(o_scaled, 1)

            def head(i, last):
                until(dve, bias_loaded, (i + 1) * 16)
                step.do(dve.tensor_tensor(tiles(bias_diag[:, :]), tiles(bias_all[:, :]),
                                          far[:, :].unsqueeze(1).to_broadcast([P, NT, P]), ALU.add))
                for q in range(NT):
                    w, d = q * P, slice(q * P, (q + 1) * P)
                    until(dve, scores_done, i * NT + q + 1)
                    until(dve, probs_ready, i * NT + q)
                    if q:
                        step.do(dve.tensor_tensor_reduce(logit[:, 0:w], ps[:, 0:w], bias_all[:, 0:w], 1.0, FAR, ALU.add,
                                                         ALU.max, off_max[:, q:q + 1]))
                    step.after()
                    first = off_max[:, q:q + 1] if q else FAR
                    step.do(dve.tensor_tensor_reduce(logit[:, d], ps[:, d], bias_diag[:, d], 1.0, first, ALU.add,
                                                     ALU.max, row_max[:, q:q + 1]))
                    step.after()
                    dve.tensor_scalar(neg_max[:, q:q + 1], row_max[:, q:q + 1], -1.0, None,
                                      ALU.mult).then_inc(logits_ready, 1)
                    if not last and q in (3, 4):
                        gate(i + 1, q - 3)
                    if q >= 2:
                        scale(i, q - 2)
                scale(i, NT - 2)
                scale(i, NT - 1)
                until(dve, o_turned, i + 1)
                until(dve, g_ready, i + 1)
                until(dve, y_stored, i * 16)
                for half in range(2):
                    t = slice(half * HALF, (half + 1) * HALF)
                    dve.tensor_tensor(yT[:, t], pm[:, t], gT[:, t], ALU.mult).then_inc(y_ready, 1)
                step.restart()
            turns(dve, FOX_H, head)

        @block.tensor
        def _(pe):
            pe.passed = t_q

            def portion(i, p):
                j, half = p // 2, p % 2
                read = (q_ready, (i - 1) * 2 + half + 1) if j == 0 else (free[j], i * 2 + half + 1)
                if j == 0 and isinstance(i, int) and i == 0:
                    read = None
                slab.portion(pe, i * S + j, j % 2, half, read)

            for p in range(2 * S):
                portion(0, p)

            def turn_probs(i, q):
                until(pe, probs_ready, i * NT + q + 1)
                until(pe, probT_ready, i * NT + q)
                if q == 0:
                    until(pe, v_ready, i + 1)
                for s in range(q + 1):
                    mm = pe.transpose(pt[:, s * P:(s + 1) * P], prob[:, s * P:(s + 1) * P], core.ident[:, :])
                mm.then_inc(probs_turned, 1)

            def times_v(i, q):
                until(pe, probT_ready, i * NT + q + 1)
                if q >= 2:
                    until(pe, o_scaled, i * NT + q - 1)
                else:
                    until(pe, y_ready, i * 2)
                out = pm[:, (q % 2) * HALF:(q % 2) * HALF + P]
                for s in range(q + 1):
                    mm = pe.matmul(out, probT[:, s * P:(s + 1) * P], v[:, s * P:(s + 1) * P],
                                   start=(s == 0), stop=(s == q))
                mm.then_inc(pv_done, 1)

            def head(i, last):
                until(pe, vT_ready, (i + 1) * 2)
                until(pe, probT_ready, i * NT)
                for c in range(NT):
                    mm = pe.transpose(pt[:, c * P:(c + 1) * P], vT[:, c * P:(c + 1) * P], core.ident[:, :])
                mm.then_inc(v_turned, 1)
                for q in range(NT):
                    w = (q + 1) * P
                    if q == 0:
                        until(pe, k_ready, i + 1)
                    if q % 4 == 0:
                        until(pe, q_ready, i * 2 + q // 4 + 1)
                    until(pe, logits_ready, i * NT + q)
                    for s in range(0, w, HALF):
                        end = min(s + HALF, w)
                        mm = pe.matmul(ps[:, s:end], qT[:, q * P:(q + 1) * P], kT[:, s:end], start=True, stop=True)
                    mm.then_inc(scores_done, 1)
                    if q:
                        turn_probs(i, q - 1)
                    if not last:
                        portion(i + 1, q)
                    if q:
                        times_v(i, q - 1)
                turn_probs(i, NT - 1)
                times_v(i, NT - 1)
                until(pe, o_scaled, (i + 1) * NT)
                for c in range(NT):
                    mm = pe.transpose(pm[:, c * P:(c + 1) * P], o_nat[:, c * P:(c + 1) * P], core.ident[:, :])
                mm.then_inc(o_turned, 1)
            turns(pe, FOX_H, head)




def ssd_phase(core, g, even_w_in, conv_w, conv_b, d_skip, ssd_norm_w):
    with Phase(core, f"ssd{g}") as ph:
        nc = core.nc
        slab = Slabs(ph, None, rows_of(even_w_in))
        ps, pt, pm = core.ps, core.pt, core.pm
        PAIRS, TAIL = GROUP_SLABS, SSD_TAPS - 1
        HEAD0 = g * PAIRS * 2
        x_in = ph.sb("x_in", [P, TAIL + T])
        (conv, sig, bT, cT, b_nat, cb, x_new, xT, x_nat, xd, xdd, state, z_new, zT, zsig, sumsq, sqr) = (
            ph.sb(n, [P, T]) for n in
            "conv sig bT cT b_nat cb x_new xT x_nat xd xdd state z_new zT zsig sumsq sqr".split())
        y_nat = xdd
        decay = [ph.sb(f"decay{h}", [P, T]) for h in range(2)]
        acum_all = [ph.sb(f"acum_all{h}", [P, T]) for h in range(2)]
        y_all = ph.sb("y_all", [P, PAIRS, T])
        CONVS = PAIRS + 2
        taps, cbias = ph.sb("taps", [P, CONVS, SSD_TAPS]), ph.sb("cbias", [P, CONVS])
        skip, nw, power = ph.sb("skip", [P, PAIRS]), ph.sb("nw", [P, PAIRS]), ph.sb("power", [P, 1])
        (small, zeroed, acum_loaded, xin_ready, conv_ready, sig_ready, bc_ready, x_new_ready, xT_ready, x_turned,
         x_nat_ready, xdd_ready, diff_ready, exp_ready, decay_ready, b_turned, b_nat_ready, cb_done, cb_ready,
         sums_done, state_ready, y_done, y_nat_ready, y_turned, y_ready, zsig_ready, z_new_ready, z_ready,
         sqr_ready, sumsq_ready, total_done, mean_ready, rstd_ready, out_ready, y_stored) = ph.sems(
            "small zeroed acum_loaded xin_ready conv_ready sig_ready bc_ready x_new_ready xT_ready x_turned "
            "x_nat_ready xdd_ready diff_ready exp_ready decay_ready b_turned b_nat_ready cb_done cb_ready "
            "sums_done state_ready y_done y_nat_ready y_turned y_ready zsig_ready z_new_ready z_ready "
            "sqr_ready sumsq_ready total_done mean_ready rstd_ready out_ready y_stored")
        (a_s, v_s, g_s, t_s, s_s), (a_q, v_q, g_q, t_q, s_q) = ph.own()
        xcol, zcol = COL_X + g * PAIRS * P, COL_Z + g * PAIRS * P
        by_head = lambda ap: ap.rearrange("p (c h d) -> p c h d", c=NT, h=2)

        def pair_of(tile, i):
            return tile[:, :, cols(i * 2 + HEAD0, 2)].unsqueeze(3).to_broadcast([P, NT, 2, SSD_P])
        block = ph.open_block()

        @block.sync
        def _(sp):
            sp.passed = s_q
            count = 0
            with nc.allow_non_contiguous_dma(reason="per-channel parameters, a few kilobytes"):
                for at, c0, n in ((0, COL_B - COL_X + g * P, 1), (1, COL_C - COL_X + g * P, 1), (2, g * PAIRS * P, PAIRS)):
                    for k in range(SSD_TAPS):
                        sp.dma_start(taps[:, at:at + n, k],
                                     conv_w[k, c0:c0 + n * P].rearrange("(s p) -> p s", p=P)).then_inc(small, 16)
                    sp.dma_start(cbias[:, at:at + n], conv_b[c0:c0 + n * P].rearrange("(s p) -> p s", p=P)).then_inc(small, 16)
                    count += SSD_TAPS + 1
                ch = slice(g * PAIRS * P, (g + 1) * PAIRS * P)
                sp.dma_start(nw[:, :], ssd_norm_w[ch].rearrange("(s p) -> p s", p=P)).then_inc(small, 16)
                for h in range(2):
                    sp.dma_start(skip[h * SSD_P:(h + 1) * SSD_P, :],
                                 d_skip[HEAD0 + h:HEAD0 + 2 * PAIRS:2].partition_broadcast(SSD_P)).then_inc(small, 16)
            assert (count + 3) * 16 == SMALL

            def load_acum(i):
                for h in range(2):
                    row = core.ssd_rows[cols(i * 2 + (HEAD0 + h), 1), :].rearrange("a t -> (a t)")
                    sp.dma_start(acum_all[h][:, :], row.partition_broadcast(P)).then_inc(acum_loaded, 16)
            load_acum(0)

            def pair(i, last):
                if not last:
                    until(sp, diff_ready, (i + 1) * 2)
                    load_acum(i + 1)
            turns(sp, PAIRS, pair)
            for s in range(PAIRS):
                sp.wait_ge(out_ready, s + 1)
                sp.dma_start(core.y_dram[FOX_H + g * PAIRS + s, :, :], y_all[:, s, :]).then_inc(y_stored, 16)
            sp.wait_ge(y_stored, 16 * PAIRS)

        @block.gpsimd
        def _(pool):
            pool.passed = g_q
            pool.memset(x_in[:, 0:TAIL], 0.0).then_inc(zeroed, 1)
            pool.memset(sumsq[:, :], 0.0).then_inc(zeroed, 1)
            pool.memset(power[:, :], -0.5).then_inc(zeroed, 1)
            for n in range(5):
                slab.split_lo(pool, n, n % 2)

            def pair(i, last):
                until(pool, x_new_ready, i + 1)
                until(pool, y_ready, i)
                pool.tensor_copy(xT[:, :], x_new[:, :]).then_inc(xT_ready, 1)
                until(pool, z_new_ready, (i + 1) * 2)
                pool.tensor_copy(zT[:, :], z_new[:, :]).then_inc(z_ready, 1)
                if not last:
                    for j in range(2):
                        slab.split_lo(pool, i * 2 + (5 + j), (1 + j) % 2)
                until(pool, sqr_ready, i + 1)
                until(pool, sumsq_ready, i)
                pool.tensor_tensor(sumsq[:, :], sumsq[:, :], sqr[:, :], ALU.add).then_inc(sumsq_ready, 1)
            pool.wait_ge(zeroed, 3)
            turns(pool, PAIRS, pair)
            for half in range(2):
                t = slice(half * HALF, (half + 1) * HALF)
                pool.wait_ge(mean_ready, half + 1)
                pool.tensor_tensor(conv[:, t], sig[:, t], power[:, :].to_broadcast([P, HALF]),
                                   ALU.pow).then_inc(rstd_ready, 1)

        @block.scalar
        def _(act):
            act.passed = a_q
            until(act, zeroed, 3)

            def evac_conv(m, n, half):
                until(act, slab.done[half], n + 1)
                until(act, conv_ready, m)
                act.activation(x_in[:, TAIL + half * HALF:TAIL + (half + 1) * HALF], core.proj[half][:, :],
                               ACT.Copy).then_inc(xin_ready, 1)

            def sigmoid(m):
                until(act, conv_ready, m + 1)
                act.activation(sig[:, :], conv[:, :], ACT.Sigmoid).then_inc(sig_ready, 1)

            def evac_z(i, n, half):
                t = slice(half * HALF, (half + 1) * HALF)
                until(act, slab.done[half], n + 1)
                until(act, z_new_ready, i * 2)
                act.activation(zsig[:, t], core.proj[half][:, :], ACT.Sigmoid).then_inc(zsig_ready, 1)

            first = [COL_B + g * P, COL_C + g * P, xcol, zcol, xcol + P, zcol + P]
            slab.load(act, 0, 0, first[0])
            slab.load(act, 1, 1, first[1])
            slab.split_hi(act, 0, 0)
            for n in range(4):
                slab.split_hi(act, n + 1, (n + 1) % 2)
                slab.load(act, n + 2, n % 2, first[n + 2])
                for half in range(2):
                    if n < 3:
                        evac_conv(n, n, half)
                    else:
                        evac_z(0, n, half)
                if n < 3:
                    sigmoid(n)
            act.wait_ge(b_turned, 1)
            act.activation(b_nat[:, :], pt[:, :], ACT.Copy).then_inc(b_nat_ready, 1)

            def pair(i, last):
                until(act, x_turned, i + 1)
                act.activation(x_nat[:, :], pt[:, :], ACT.Copy).then_inc(x_nat_ready, 1)
                for h in range(2):
                    until(act, diff_ready, i * 2 + h + 1)
                    act.activation(decay[h][:, :], decay[h][:, :], ACT.Exp).then_inc(exp_ready, 1)
                if not last:
                    i2 = (i + 2) % PAIRS
                    n = i * 2 + 4
                    slab.split_hi(act, n + 1, 1, i + 2)
                    slab.load(act, n + 2, 0, i2 * P + xcol)
                    evac_conv(i + 3, n, 0)
                    evac_conv(i + 3, n, 1)
                    sigmoid(i + 3)
                    slab.split_hi(act, n + 2, 0, i + 3)
                    slab.load(act, n + 3, 1, i2 * P + zcol)
                    evac_z(i + 1, n + 1, 0)
                    evac_z(i + 1, n + 1, 1)
                until(act, y_ready, i + 1)
                until(act, sumsq_ready, i)
                act.activation(sqr[:, :], y_all[:, cols(i, 1), :].rearrange("p a t -> p (a t)"),
                               ACT.Square).then_inc(sqr_ready, 1)
            turns(act, PAIRS, pair)
            for b in range(2):
                act.wait_ge(slab.loaded[b], 16 * (PAIRS + 2))

        @block.vector
        def _(dve):
            dve.passed = v_q
            step = Steps(dve, v_s)
            dve.wait_ge(small, SMALL)

            def convolve(m, used, count):
                until(dve, xin_ready, (m + 1) * 2)
                until(dve, used, count)
                w = lambda k: taps[:, cols(m, 1), k]
                step.do(dve.tensor_scalar(conv[:, :], x_in[:, TAIL:TAIL + T], w(TAIL), cbias[:, cols(m, 1)],
                                          ALU.mult, ALU.add))
                for k in range(TAIL):
                    step.after()
                    ins = dve.scalar_tensor_tensor(out=conv[:, :], in0=x_in[:, k:k + T], scalar=w(k),
                                                   in1=conv[:, :], op0=ALU.mult, op1=ALU.add)
                    if k < TAIL - 1:
                        step.do(ins)
                ins.then_inc(conv_ready, 1)

            def silu(m, out, ready):
                until(dve, sig_ready, m + 1)
                dve.tensor_tensor(out[:, :], conv[:, :], sig[:, :], ALU.mult).then_inc(ready, 1)

            def gate(i, half):
                t = slice(half * HALF, (half + 1) * HALF)
                until(dve, zsig_ready, i * 2 + half + 1)
                until(dve, z_ready, i)
                dve.tensor_tensor(z_new[:, t], core.proj[half][:, :], zsig[:, t], ALU.mult).then_inc(z_new_ready, 1)

            convolve(0, bc_ready, 0)
            silu(0, bT, bc_ready)
            convolve(1, bc_ready, 1)
            silu(1, cT, bc_ready)
            convolve(2, bc_ready, 2)
            silu(2, x_new, x_new_ready)
            dve.wait_ge(cb_done, 1)
            dve.tensor_tensor(tiles(cb[:, :]), tiles(ps[:, :]), core.tri[:, :].unsqueeze(1).to_broadcast([P, NT, P]),
                              ALU.mult).then_inc(cb_ready, 1)
            dve.wait_ge(cb_ready, 1)
            gate(0, 0)
            gate(0, 1)
            step.restart()

            def pair(i, last):
                until(dve, acum_loaded, (i + 1) * 32)
                for h in range(2):
                    a = core.acum[:, :, cols(i * 2 + (HEAD0 + h), 1)].to_broadcast([P, NT, P])
                    step.do(dve.tensor_tensor(tiles(decay[h][:, :]), tiles(acum_all[h][:, :]), a, ALU.subtract))
                for h in range(2):
                    step.after(h + 1)
                    dve.tensor_scalar(decay[h][:, :], decay[h][:, :], 0.0, None, ALU.min).then_inc(diff_ready, 1)
                until(dve, x_nat_ready, i + 1)
                dve.tensor_tensor(by_head(xdd[:, :]), by_head(x_nat[:, :]), pair_of(core.state_dec, i),
                                  ALU.mult).then_inc(xdd_ready, 1)
                step.do(dve.tensor_tensor(by_head(xd[:, :]), by_head(x_nat[:, :]), pair_of(core.dt, i), ALU.mult))
                for h in range(2):
                    until(dve, exp_ready, i * 2 + h + 1)
                    dve.tensor_tensor(decay[h][:, :], decay[h][:, :], cb[:, :], ALU.mult).then_inc(decay_ready, 1)
                until(dve, sums_done, i + 1)
                step.do(dve.tensor_copy(state[:, P:2 * P], pm[:, 0:P]))
                for c in range(1, NT - 1):
                    step.after()
                    for h in range(2):
                        now, nxt = c * P + h * SSD_P, (c + 1) * P + h * SSD_P
                        ins = dve.scalar_tensor_tensor(
                            out=state[:, nxt:nxt + SSD_P], in0=state[:, now:now + SSD_P],
                            scalar=core.chunk_dec[:, c, cols(i * 2 + (HEAD0 + h), 1)],
                            in1=pm[:, now:now + SSD_P], op0=ALU.mult, op1=ALU.add)
                        if c < NT - 2 or h == 0:
                            step.do(ins)
                ins.then_inc(state_ready, 1)
                if not last:
                    until(dve, xT_ready, i + 1)
                    convolve(i + 3, x_new_ready, i + 1)
                    silu(i + 3, x_new, x_new_ready)
                until(dve, y_done, i + 1)
                rest = lambda ap: by_head(ap)[:, 1:NT, :, :]
                step.do(dve.tensor_tensor(rest(y_nat[:, :]), rest(ps[:, :]), pair_of(core.out_dec, i)[:, 1:NT, :, :],
                                          ALU.mult))
                step.do(dve.tensor_copy(y_nat[:, 0:P], pt[:, 0:P]))
                step.after()
                dve.tensor_tensor(y_nat[:, P:T], y_nat[:, P:T], pt[:, P:T], ALU.add).then_inc(y_nat_ready, 1)
                if not last:
                    gate(i + 1, 0)
                until(dve, y_turned, i + 1)
                step.do(dve.scalar_tensor_tensor(out=x_nat[:, :], in0=xT[:, :], scalar=skip[:, cols(i, 1)],
                                                 in1=pm[:, :], op0=ALU.mult, op1=ALU.add))
                until(dve, z_ready, i + 1)
                step.after()
                dve.tensor_tensor(y_all[:, cols(i, 1), :].rearrange("p a t -> p (a t)"), x_nat[:, :], zT[:, :],
                                  ALU.mult).then_inc(y_ready, 1)
                if not last:
                    gate(i + 1, 1)
                step.restart()
            turns(dve, PAIRS, pair)
            dve.wait_ge(total_done, 1)
            for half in range(2):
                t = slice(half * HALF, (half + 1) * HALF)
                dve.tensor_scalar(sig[:, t], ps[:, t], 1.0 / (PAIRS * P), EPS, ALU.mult, ALU.add).then_inc(mean_ready, 1)
            dve.wait_ge(rstd_ready, 2)
            for s in range(PAIRS):
                dve.scalar_tensor_tensor(out=y_all[:, s, :], in0=y_all[:, s, :], scalar=nw[:, s:s + 1], in1=conv[:, :],
                                         op0=ALU.mult, op1=ALU.mult).then_inc(out_ready, 1)

        @block.tensor
        def _(pe):
            pe.passed = t_q

            def turn(bank, src, ready):
                for c in range(NT):
                    mm = pe.transpose(bank[:, c * P:(c + 1) * P], src[:, c * P:(c + 1) * P], core.ident[:, :])
                mm.then_inc(ready, 1)

            for n in range(3):
                for half in range(2):
                    slab.portion(pe, n, n % 2, half, (xin_ready, (n - 1) * 2 + half + 1) if n else None)
            pe.wait_ge(bc_ready, 1)
            turn(pt, bT, b_turned)
            pe.wait_ge(bc_ready, 2)
            for c in range(NT):
                t = slice(c * P, (c + 1) * P)
                mm = pe.matmul(ps[:, t], bT[:, t], cT[:, t], start=True, stop=True)
            mm.then_inc(cb_done, 1)
            for half in range(2):
                slab.portion(pe, 3, 1, half, (xin_ready, 2 * 2 + half + 1))

            def pair(i, last):
                def portion(j, half):
                    if not last:
                        free = (z_new_ready, i * 2 + half + 1) if j == 0 else (xin_ready, (i + 3) * 2 + half + 1)
                        slab.portion(pe, i * 2 + (4 + j), j, half, free)

                until(pe, xT_ready, i + 1)
                pe.wait_ge(b_nat_ready, 1)
                turn(pt, xT, x_turned)
                portion(0, 0)
                until(pe, xdd_ready, i + 1)
                for c in range(NT - 1):
                    t = slice(c * P, (c + 1) * P)
                    mm = pe.matmul(pm[:, t], b_nat[:, t], xdd[:, t], start=True, stop=True)
                mm.then_inc(sums_done, 1)
                portion(0, 1)
                until(pe, decay_ready, (i + 1) * 2)
                until(pe, state_ready, i + 1)
                until(pe, cb_ready, 1)
                for c in range(NT):
                    t = slice(c * P, (c + 1) * P)
                    if c:
                        pe.matmul(ps[:, t], cT[:, t], state[:, t], start=True, stop=True)
                    for h in range(2):
                        th = slice(c * P + h * SSD_P, c * P + (h + 1) * SSD_P)
                        mm = pe.matmul(pt[:, th], decay[h][:, t], xd[:, th], start=True, stop=True)
                mm.then_inc(y_done, 1)
                portion(1, 0)
                until(pe, y_nat_ready, i + 1)
                turn(pm, y_nat, y_turned)
                portion(1, 1)
            turns(pe, PAIRS, pair)
            pe.wait_ge(sumsq_ready, PAIRS)
            for half in range(2):
                t = slice(half * HALF, (half + 1) * HALF)
                mm = pe.matmul(ps[:, t], core.ones[:, :], sumsq[:, t], start=True, stop=True)
            mm.then_inc(total_done, 1)


SMALL = 16 * (3 * (SSD_TAPS + 1) + 3)


def out_phase(core, name, w_out, h_dram, final_w, dst):
    with Phase(core, name) as ph:
        nc = core.nc
        final = final_w is not None
        w_hi = ph.sb("w_hi", [P, YT, D], F32R)
        w_lo = core.uT[:, :, :, :].rearrange("p a k t -> p (a k) t")
        y_raw = ph.sb("y_raw", [P, YT, P])
        y_hi, y_lo = ([ph.sb(f"{n}{b}", [P, YT, P], F32R) for b in range(2)] for n in ("y_hi", "y_lo"))
        w_raw, h_old, h_new = ([ph.sb(f"{n}{b}", [P, D]) for b in range(2)] for n in ("w_raw", "h_old", "h_new"))
        w_all = ph.sb("w_all", [P, D]) if final else None
        sumsq, mean, rstd = (ph.sb(n, [P, 2]) for n in ("sumsq", "mean", "rstd"))
        power = ph.sb("power", [P, 1])
        banks = [core.ps, core.pt]
        (w0, w1, h0, h1, s0, s1, small, y_loaded, w_hi_ready, w_lo_ready, y_hi_ready, y_lo_ready, done, h_ready,
         sq_ready, rstd_ready, out_ready, power_set) = ph.sems(
            "w0_loaded w1_loaded h0_loaded h1_loaded stored0 stored1 small y_loaded w_hi_ready w_lo_ready "
            "y_hi_ready y_lo_ready done h_ready sq_ready rstd_ready out_ready power_set")
        w_loaded, h_loaded, stored = (w0, w1), (h0, h1), (s0, s1)
        (a_s, v_s, g_s, t_s, s_s), (a_q, v_q, g_q, t_q, s_q) = ph.own()
        PAIRS = NT // 2
        block = ph.open_block()

        @block.sync
        def _(sp):
            sp.passed = s_q
            if final:
                sp.dma_start(w_all[:, :], final_w.partition_broadcast(P)).then_inc(small, 16)
            with sp.Fori(0, PAIRS) as pair:
                for b in range(2):
                    t = pair * 2 + b
                    until(sp, y_lo_ready, t)
                    sp.dma_start(y_raw[:, :, :], core.y_dram[:, :, cols(t * P, P)].rearrange("k p t -> p k t")
                                 ).then_inc(y_loaded, 16)
                    until(sp, sq_ready if final else h_ready, t + 1)
                    sp.dma_start(h_old[b][:, :], h_dram[cols(t * P, P), :]).then_inc(h_loaded[b], 16)

        @block.gpsimd
        def _(pool):
            pool.passed = g_q
            pool.memset(power[:, :], -0.5).then_inc(power_set, 1)
            for b in range(2):
                pool.dma_start(w_raw[b][:, :], w_out[b * P:(b + 1) * P, :]).then_inc(w_loaded[b], 16)
            with pool.Fori(0, YT // 2 - 1) as pair:
                for b in range(2):
                    k = pair * 2 + b
                    until(pool, w_lo_ready, k + 1)
                    pool.dma_start(w_raw[b][:, :], w_out[cols((k + 2) * P, P), :]).then_inc(w_loaded[b], 16)
            pool.wait_ge(power_set, 1)
            step = Steps(pool, g_s)
            with pool.Fori(0, PAIRS) as pair:
                for b in range(2):
                    t = pair * 2 + b
                    if final:
                        until(pool, sq_ready, t + 3)
                        step.do(pool.tensor_scalar(mean[:, b:b + 1], sumsq[:, b:b + 1], 1.0 / D, EPS, ALU.mult, ALU.add))
                        step.after()
                        pool.tensor_tensor(rstd[:, b:b + 1], mean[:, b:b + 1], power[:, :], ALU.pow).then_inc(rstd_ready, 1)
                        until(pool, out_ready, t + 1)
                    else:
                        until(pool, h_ready, t + 3)
                    pool.dma_start(dst[cols(t * P, P), :], h_new[b][:, :]).then_inc(stored[b], 16)
                step.restart()
            for b in range(2):
                pool.wait_ge(stored[b], 16 * PAIRS)

        @block.scalar
        def _(act):
            act.passed = a_q
            if final:
                act.sem_inc(sq_ready, 2)

            def split_y(t, b):
                until(act, y_loaded, (t + 1) * 16)
                until(act, done, t + 1)
                act.activation(y_hi[b][:, :, :], y_raw[:, :, :], ACT.Copy).then_inc(y_hi_ready, 1)

            split_y(0, 0)
            with act.Fori(0, YT // 2) as pair:
                for b in range(2):
                    k = pair * 2 + b
                    until(act, w_loaded[b], (pair + 1) * 16)
                    act.activation(w_hi[:, cols(k, 1), :].rearrange("p a n -> p (a n)"), w_raw[b][:, :],
                                   ACT.Copy).then_inc(w_hi_ready, 1)

            def two(pair, last):
                for b in range(2):
                    t = pair * 2 + b
                    if not (last and b == 1):
                        split_y(t + 1, 1 - b)
                    if final:
                        until(act, h_ready, t + 3)
                        act.activation(h_old[b][:, :], h_new[b][:, :], ACT.Square,
                                       accum_out=sumsq[:, b:b + 1]).then_inc(sq_ready, 1)
            turns(act, PAIRS, two)

        @block.vector
        def _(dve):
            dve.passed = v_q
            dve.sem_inc(h_ready, 2)

            def split_y(t, b):
                until(dve, y_hi_ready, t + 1)
                dve.tensor_tensor(y_lo[b][:, :, :], y_raw[:, :, :], y_hi[b][:, :, :].bitcast(F32),
                                  ALU.subtract).then_inc(y_lo_ready, 1)

            split_y(0, 0)
            with dve.Fori(0, YT // 2) as pair:
                for b in range(2):
                    k = pair * 2 + b
                    until(dve, w_hi_ready, k + 1)
                    dve.tensor_tensor(w_lo[:, cols(k, 1), :].rearrange("p a n -> p (a n)"), w_raw[b][:, :],
                                      w_hi[:, cols(k, 1), :].rearrange("p a n -> p (a n)").bitcast(F32),
                                      ALU.subtract).then_inc(w_lo_ready, 1)
            if final:
                dve.wait_ge(small, 16)

            def two(pair, last):
                for b in range(2):
                    t = pair * 2 + b
                    if not (last and b == 1):
                        split_y(t + 1, 1 - b)
                    until(dve, done, t + 3)
                    until(dve, h_loaded[b], (pair + 1) * 16)
                    until(dve, stored[b], pair * 16)
                    dve.tensor_tensor(h_new[b][:, :], banks[b][:, :], h_old[b][:, :], ALU.add).then_inc(h_ready, 1)
                    if final:
                        until(dve, rstd_ready, t + 1)
                        dve.scalar_tensor_tensor(out=h_new[b][:, :], in0=h_new[b][:, :], scalar=rstd[:, b:b + 1],
                                                 in1=w_all[:, :], op0=ALU.mult, op1=ALU.mult).then_inc(out_ready, 1)
            turns(dve, PAIRS, two)

        @block.tensor
        def _(pe):
            pe.passed = t_q
            pe.sem_inc(done, 2)

            with pe.Fori(0, PAIRS) as pair:
                for b in range(2):
                    t = pair * 2 + b
                    until(pe, y_lo_ready, t + 1)
                    until(pe, h_ready, t + 1)
                    for k in range(YT):
                        pe.wait_ge(w_lo_ready, k + 1)
                        ends = dict(start=(k == 0), stop=False), dict(start=False, stop=(k == YT - 1))
                        halves = [slice(h * HALF, (h + 1) * HALF) for h in range(2)]
                        for h in halves:
                            pe.matmul(banks[b][:, h], y_hi[b][:, k, :], w_hi[:, k, h], **ends[0])
                        for h in halves:
                            pe.matmul(banks[b][:, h], y_hi[b][:, k, :], w_lo[:, k, h], start=False, stop=False)
                        for h in halves:
                            mm = pe.matmul(banks[b][:, h], y_lo[b][:, k, :], w_hi[:, k, h], **ends[1])
                    mm.then_inc(done, 1)


def hgrn_phase(core, odd_w_in, lb_logits, norm_w):
    with Phase(core, "hgrn") as ph:
        nc = core.nc
        slab = Slabs(ph, None, rows_of(odd_w_in))
        ps, pt, pm = core.ps, core.pt, core.pm
        qT, kT, fT, halves_prod, scores, vT, v, k_nat, state, o_nat, sig, sqr, g_new, gT, yT = (
            ph.sb(n, [P, T]) for n in
            "qT kT fT halves_prod scores vT v k_nat state o_nat sig sqr g_new gT yT".split())
        diag = ph.sb("diag", [P, T], mybir.dt.int8)
        masks = ph.sb("masks", [P, len(LEVELS), HALF], mybir.dt.int8)
        lb, rest, lb_tmp, lb_inv = (ph.sb(n, [P, HG_H]) for n in ("lb", "rest", "lb_tmp", "lb_inv"))
        nw, power = ph.sb("nw", [P, 1]), ph.sb("power", [P, NT])
        sumsq, mean, rstd = (ph.sb(n, [P, NT]) for n in ("sumsq", "mean", "rstd"))
        (small, made, lb_diff, lb_exp, vT_ready, v_turned, v_ready, sig_ready, g_new_ready, g_ready, f_raw_ready,
         f_ready, q_ready, level_done, level_ready, scores_ready, k_turned, k_nat_ready, sums_done, state_ready,
         o_done, sq_ready, sumsq_ready, rstd_ready, o_nat_ready, o_turned, y_ready, y_stored, qsig_ready) = ph.sems(
            "small made lb_diff lb_exp vT_ready v_turned v_ready sig_ready g_new_ready g_ready f_raw_ready "
            "f_ready q_ready level_done level_ready scores_ready k_turned k_nat_ready sums_done state_ready "
            "o_done sq_ready sumsq_ready rstd_ready o_nat_ready o_turned y_ready y_stored qsig_ready")
        (a_s, v_s, g_s, t_s, s_s), (a_q, v_q, g_q, t_q, s_q) = ph.own()
        COLS = [2 * HG_W, 3 * HG_W, HG_W, 0]
        S, L = len(COLS), len(LEVELS) + 1
        prod = {1: fT[:, :]}
        at = 0
        for h in LEVELS:
            prod[2 * h] = halves_prod[:, at:at + T // (2 * h)]
            at += T // (2 * h)
        block = ph.open_block()

        def side(ap, h, right):
            return ap.rearrange("p (b two h) -> p b two h", two=2, h=h)[:, :, int(right), :]

        @block.sync
        def _(sp):
            sp.passed = s_q
            with nc.allow_non_contiguous_dma(reason="per-channel parameters, a few kilobytes"):
                sp.dma_start(lb[:, :], lb_logits[0, :].rearrange("(h k) -> k h", k=P)).then_inc(small, 16)
                sp.dma_start(nw[:, :], norm_w.rearrange("(v a) -> v a", a=1)).then_inc(small, 16)
            with sp.Fori(0, HG_H) as i:
                until(sp, y_ready, (i + 1) * 2)
                sp.dma_start(core.y_dram[cols(i, 1), :, :].rearrange("a p t -> p (a t)"), yT[:, :]).then_inc(y_stored, 16)
            sp.wait_ge(y_stored, 16 * HG_H)

        @block.gpsimd
        def _(pool):
            pool.passed = g_q
            pool.memset(scores[:, :], 0.0).then_inc(made, 1)
            pool.memset(power[:, :], -0.5).then_inc(made, 1)
            pool.memset(diag[:, :], 0.0).then_inc(made, 1)
            pool.memset(masks[:, :, :], 1.0).then_inc(made, 1)
            pool.wait_ge(made, 4)
            pool.affine_select(out=diag[:, :], in_=diag[:, :], compare_op=ALU.not_equal, fill=1.0, base=0,
                               pattern=[[0, NT], [-1, P]], channel_multiplier=1).then_inc(made, 1)
            for j, h in enumerate(LEVELS):
                n = P // (2 * h)
                pool.affine_select(out=masks[:, j, :], in_=masks[:, j, :], compare_op=ALU.is_ge, fill=0.0, base=0,
                                   pattern=[[0, NT], [-2 * h, n], [0, h]], channel_multiplier=1).then_inc(made, 1)
            pool.wait_ge(made, 5 + len(LEVELS))
            for j, h in enumerate(LEVELS):
                n = P // (2 * h)
                pool.affine_select(out=masks[:, j, :], in_=masks[:, j, :], compare_op=ALU.is_ge, fill=0.0, base=h - 1,
                                   pattern=[[0, NT], [2 * h, n], [0, h]], channel_multiplier=-1).then_inc(made, 1)
            for n in range(S + 1):
                slab.split_lo(pool, n, n % 2)
            step = Steps(pool, g_s)

            def head(i, last):
                until(pool, g_new_ready, (i + 1) * 2)
                until(pool, y_ready, i * 2)
                pool.tensor_copy(gT[:, :], g_new[:, :]).then_inc(g_ready, 1)
                if not last:
                    for j in range(3):
                        slab.split_lo(pool, (i + 1) * S + j + 1, (j + 1) % 2)
                until(pool, sumsq_ready, i + 1)
                step.do(pool.tensor_scalar(mean[:, :], sumsq[:, :], 1.0 / P, EPS, ALU.mult, ALU.add))
                step.after()
                pool.tensor_tensor(rstd[:, :], mean[:, :], power[:, :], ALU.pow).then_inc(rstd_ready, 1)
                if not last:
                    slab.split_lo(pool, (i + 1) * S + 4, 0)
                step.restart()
            turns(pool, HG_H, head)

        @block.scalar
        def _(act):
            act.passed = a_q

            def ahead(i, j):
                n = i * S + j
                slab.split_hi(act, n + 1, (j + 1) % 2, i * (S // 2) + (j + 1) // 2)
                h2 = (i + (j + 2) // S) % HG_H
                slab.load(act, n + 2, j % 2, h2 * P + COLS[(j + 2) % S])

            def evacuate(i, p):
                j, half = p // 2, p % 2
                t, bank = slice(half * HALF, (half + 1) * HALF), core.proj[half][:, :]
                until(act, slab.done[half], i * S + j + 1)
                if j == 0:
                    until(act, v_turned, i)
                    act.activation(vT[:, t], bank, ACT.Copy).then_inc(vT_ready, 1)
                elif j == 1:
                    until(act, q_ready, i * 2)
                    act.activation(sig[:, t], bank, ACT.Sigmoid).then_inc(sig_ready, 1)
                elif j == 2:
                    until(act, scores_ready, i)
                    act.activation(fT[:, t], bank, ACT.Sigmoid).then_inc(f_raw_ready, 1)
                    act.activation(kT[:, t], bank, ACT.Sigmoid, scale=-1.0).then_inc(f_raw_ready, 1)
                else:
                    until(act, g_new_ready, (i + 1) * 2)
                    act.activation(sig[:, t], bank, ACT.Sigmoid).then_inc(qsig_ready, 1)

            slab.load(act, 0, 0, COLS[0])
            slab.load(act, 1, 1, COLS[1])
            slab.split_hi(act, 0, 0)
            act.wait_ge(lb_diff, 1)
            act.activation(lb_tmp[:, :], lb_tmp[:, :], ACT.Exp).then_inc(lb_exp, 1)
            for j in range(S):
                ahead(0, j)
                evacuate(0, 2 * j)
                evacuate(0, 2 * j + 1)

            def head(i, last):
                until(act, v_turned, i + 1)
                act.activation(v[:, :], pt[:, :], ACT.Copy).then_inc(v_ready, 1)
                if not last:
                    ahead(i + 1, 0)
                    evacuate(i + 1, 0)
                    evacuate(i + 1, 1)
                    ahead(i + 1, 1)
                    evacuate(i + 1, 2)
                    evacuate(i + 1, 3)
                until(act, k_turned, i + 1)
                act.activation(k_nat[:, :], pt[:, :], ACT.Copy).then_inc(k_nat_ready, 1)
                if not last:
                    ahead(i + 1, 2)
                    evacuate(i + 1, 4)
                until(act, o_done, i + 1)
                act.activation(sqr[:, :], ps[:, :], ACT.Square).then_inc(sq_ready, 1)
                if not last:
                    evacuate(i + 1, 5)
                    ahead(i + 1, 3)
                    evacuate(i + 1, 6)
                    evacuate(i + 1, 7)
            turns(act, HG_H, head)
            for b in range(2):
                act.wait_ge(slab.loaded[b], 16 * (HG_H * S // 2 + 1))

        @block.vector
        def _(dve):
            dve.passed = v_q
            step = Steps(dve, v_s)
            dve.wait_ge(small, 32)
            dve.tensor_tensor(lb_tmp[:, :], lb[:, :], lb[:, :], ALU.subtract).then_inc(lb_diff, 1)
            dve.wait_ge(lb_exp, 1)
            step.do(dve.reciprocal(lb_inv[:, :], lb_tmp[:, :]))
            step.after()
            step.do(dve.tensor_tensor(lb_tmp[:, :], lb_tmp[:, :], lb_inv[:, :], ALU.mult))
            step.after()
            step.do(dve.tensor_tensor(lb[:, :], lb_tmp[:, :], lb_tmp[:, :], ALU.subtract))
            step.after()
            step.do(dve.tensor_scalar(rest[:, :], lb[:, :], -1.0, 1.0, ALU.mult, ALU.add))
            step.restart()
            dve.wait_ge(made, 5 + 2 * len(LEVELS))

            def gate(i, half):
                t = slice(half * HALF, (half + 1) * HALF)
                until(dve, sig_ready, i * 2 + half + 1)
                until(dve, g_ready, i)
                dve.tensor_tensor(g_new[:, t], core.proj[half][:, :], sig[:, t], ALU.mult).then_inc(g_new_ready, 1)

            def bound(i, half):
                t = slice(half * HALF, (half + 1) * HALF)
                until(dve, f_raw_ready, i * 4 + half * 2 + 2)
                dve.tensor_scalar(fT[:, t], fT[:, t], rest[:, cols(i, 1)], lb[:, cols(i, 1)], ALU.mult,
                                  ALU.add).then_inc(f_ready, 1)
                dve.tensor_scalar(kT[:, t], kT[:, t], rest[:, cols(i, 1)], None, ALU.mult).then_inc(f_ready, 1)

            def silu_q(i, half):
                t = slice(half * HALF, (half + 1) * HALF)
                until(dve, qsig_ready, i * 2 + half + 1)
                dve.tensor_tensor(qT[:, t], core.proj[half][:, :], sig[:, t], ALU.mult).then_inc(q_ready, 1)

            for job in (gate, bound, silu_q):
                for half in range(2):
                    job(0, half)

            def head(i, last):
                until(dve, f_ready, (i + 1) * 4)
                step.do(dve.tensor_tensor(prod[2], fT[:, 0:T:2], fT[:, 1:T:2], ALU.mult))
                until(dve, level_done, i * L + 1)
                step.do(dve.tensor_tensor(qT[:, :], qT[:, :], fT[:, :], ALU.mult))
                dve.copy_predicated(scores[:, :], diag[:, :], ps[:, :]).then_inc(level_ready, 1)
                for j, h in enumerate(LEVELS):
                    until(dve, level_done, i * L + j + 2)
                    step.after()
                    wide = [P, T // (2 * h), h]
                    left = prod[h][:, 0::2].unsqueeze(2).to_broadcast(wide)
                    right = prod[h][:, 1::2].unsqueeze(2).to_broadcast(wide)
                    step.do(dve.tensor_tensor(side(qT[:, :], h, True), side(qT[:, :], h, True), left, ALU.mult))
                    dve.tensor_tensor(side(kT[:, :], h, False), side(kT[:, :], h, False), right,
                                      ALU.mult).then_inc(level_ready, 1)
                    if 2 * h < P:
                        step.do(dve.tensor_tensor(prod[4 * h], prod[2 * h][:, 0::2], prod[2 * h][:, 1::2], ALU.mult))
                    bank = ps[:, ((j + 1) % 2) * HALF:((j + 1) % 2 + 1) * HALF].rearrange("p (b h) -> p b h", h=h)
                    ins = dve.copy_predicated(side(scores[:, :], h, True),
                                              masks[:, j, :].rearrange("p (b h) -> p b h", h=h), bank)
                    if h == LEVELS[-1]:
                        ins.then_inc(scores_ready, 1)
                    else:
                        step.do(ins)
                    if not last and j == 6:
                        gate(i + 1, 0)
                        gate(i + 1, 1)
                until(dve, sums_done, i + 1)
                step.do(dve.tensor_copy(state[:, P:2 * P], pm[:, 0:P]))
                for c in range(1, NT - 1):
                    step.after()
                    ins = dve.scalar_tensor_tensor(out=state[:, (c + 1) * P:(c + 2) * P], in0=state[:, c * P:(c + 1) * P],
                                                   scalar=prod[P][:, c:c + 1], in1=pm[:, c * P:(c + 1) * P],
                                                   op0=ALU.mult, op1=ALU.add)
                    if c < NT - 2:
                        step.do(ins)
                ins.then_inc(state_ready, 1)
                if not last:
                    bound(i + 1, 0)
                until(dve, sq_ready, i + 1)
                dve.tensor_reduce(sumsq[:, :], tiles(sqr[:, :]), AX.X, ALU.add).then_inc(sumsq_ready, 1)
                if not last:
                    bound(i + 1, 1)
                until(dve, rstd_ready, i + 1)
                dve.tensor_tensor(tiles(o_nat[:, :]), tiles(ps[:, :]), rstd[:, :].unsqueeze(2).to_broadcast([P, NT, P]),
                                  ALU.mult).then_inc(o_nat_ready, 1)
                until(dve, o_turned, i + 1)
                until(dve, g_ready, i + 1)
                until(dve, y_stored, i * 16)
                for half in range(2):
                    t = slice(half * HALF, (half + 1) * HALF)
                    dve.scalar_tensor_tensor(out=yT[:, t], in0=pt[:, t], scalar=nw[:, :], in1=gT[:, t],
                                             op0=ALU.mult, op1=ALU.mult).then_inc(y_ready, 1)
                if not last:
                    silu_q(i + 1, 0)
                    silu_q(i + 1, 1)
                step.restart()
            turns(dve, HG_H, head)

        @block.tensor
        def _(pe):
            pe.passed = t_q

            def portion(i, p, part=None):
                j, half = p // 2, p % 2
                if j == 0:
                    free = None if isinstance(i, int) and i == 0 else (q_ready, (i - 1) * 2 + half + 1)
                else:
                    free = [(vT_ready, i * 2 + half + 1), (g_new_ready, i * 2 + half + 1),
                            (f_raw_ready, i * 4 + half * 2 + 2)][j - 1]
                slab.portion(pe, i * S + j, j % 2, half, free, part)

            for p in range(2 * S):
                portion(0, p)

            def turn(bank, src, ready):
                for c in range(NT):
                    mm = pe.transpose(bank[:, c * P:(c + 1) * P], src[:, c * P:(c + 1) * P], core.ident[:, :])
                mm.then_inc(ready, 1)

            def head(i, last):
                def next_part(n):
                    if not last:
                        portion(i + 1, n // 2, n % 2)

                until(pe, vT_ready, (i + 1) * 2)
                until(pe, y_ready, i * 2)
                turn(pt, vT, v_turned)
                until(pe, q_ready, (i + 1) * 2)
                until(pe, f_ready, (i + 1) * 4)
                for c in range(NT):
                    t = slice(c * P, (c + 1) * P)
                    mm = pe.matmul(ps[:, t], kT[:, t], qT[:, t], start=True, stop=True)
                mm.then_inc(level_done, 1)
                next_part(0)
                for j, h in enumerate(LEVELS):
                    until(pe, level_ready, i * L + j + 1)
                    for c in range(NT):
                        t = slice(c * P, (c + 1) * P)
                        out = ps[:, ((j + 1) % 2) * HALF + c * (P // 2):((j + 1) % 2) * HALF + (c + 1) * (P // 2)]
                        mm = pe.matmul(out, kT[:, t], side(qT[:, t], h, True), start=True, stop=True)
                    mm.then_inc(level_done, 1)
                    next_part(j + 1)
                until(pe, level_ready, (i + 1) * L)
                until(pe, v_ready, i + 1)
                turn(pt, kT, k_turned)
                next_part(8)
                until(pe, k_nat_ready, i + 1)
                for c in range(NT - 1):
                    t = slice(c * P, (c + 1) * P)
                    mm = pe.matmul(pm[:, t], k_nat[:, t], v[:, t], start=True, stop=True)
                mm.then_inc(sums_done, 1)
                next_part(9)
                next_part(10)
                until(pe, state_ready, i + 1)
                until(pe, scores_ready, i + 1)
                for c in range(NT):
                    t = slice(c * P, (c + 1) * P)
                    mm = pe.matmul(ps[:, t], scores[:, t], v[:, t], start=True, stop=(c == 0))
                    if c:
                        mm = pe.matmul(ps[:, t], qT[:, t], state[:, t], start=False, stop=True)
                mm.then_inc(o_done, 1)
                next_part(11)
                next_part(12)
                until(pe, o_nat_ready, i + 1)
                turn(pt, o_nat, o_turned)
                for n in range(13, 16):
                    next_part(n)
            turns(pe, HG_H, head)


_INS = ["x", "norm_w", "final_norm_w", "even_w_in", "even_w_out", "fox_f_bias", "ssd_conv_w", "ssd_conv_b",
        "ssd_dt_bias", "ssd_A_log", "ssd_D", "ssd_norm_w", "odd_w_in", "odd_w_out", "hgrn_lb_logits", "hgrn_norm_w"]


def trunk(nc, x, norm_w, final_norm_w, even_w_in, even_w_out, fox_f_bias, ssd_conv_w, ssd_conv_b,
          ssd_dt_bias, ssd_A_log, ssd_D, ssd_norm_w, odd_w_in, odd_w_out, hgrn_lb_logits, hgrn_norm_w, out):
    with ExitStack() as ctx:
        core = Core(nc, ctx)
        constants(core)
        norm_phase(core, "norm0", x[0], norm_w[0])
        gates_phase(core, even_w_in[0], fox_f_bias[0], ssd_dt_bias[0], ssd_A_log[0])
        fox_phase(core, even_w_in[0])
        for g in range(SSD_G):
            ssd_phase(core, g, even_w_in[0], ssd_conv_w[0], ssd_conv_b[0], ssd_D[0], ssd_norm_w[0])
        out_phase(core, "out0", even_w_out[0], x[0], None, core.h_dram)
        norm_phase(core, "norm1", core.h_dram, norm_w[1])
        hgrn_phase(core, odd_w_in[0], hgrn_lb_logits, hgrn_norm_w[0])
        out_phase(core, "out1", odd_w_out[0], core.h_dram, final_norm_w, out[0])


def kernel(**inputs):
    import numpy as np
    import concourse.bacc as bacc
    from concourse.bass_utils import run_bass_kernel_spmd

    nc = bacc.Bacc("TRN2", target_bir_lowering=False, num_devices=1)
    arrays, args = {}, []
    for name in _INS:
        a = np.ascontiguousarray(inputs[name])
        arrays[f"in_{name}"] = a
        args.append(nc.dram_tensor(f"in_{name}", a.shape, mybir.dt.from_np(a.dtype), kind="ExternalInput").ap())
    args.append(nc.dram_tensor("out", (1, T, D), F32, kind="ExternalOutput").ap())
    trunk(nc, *args)
    result = run_bass_kernel_spmd(nc, [arrays], core_ids=[0])
    return result.results[0]["out"]
```

```python
from contextlib import ExitStack

import concourse.bass as bass
from concourse import mybir

F32 = mybir.dt.float32
F32R = mybir.dt.float32r
ALU = mybir.AluOpType
ACT = mybir.ActivationFunctionType
AX = mybir.AxisListType

P = 128
T = 1024
D = 1024
KT = D // P
NT = T // P
HALF = T // 2
MIX = 2 * D
YT = MIX // P
EPS = 1e-5
FOX_H, FOX_D, FOX_W = 8, 128, 1024
SSD_H, SSD_P, SSD_W, SSD_G, SSD_N, SSD_TAPS = 16, 64, 1024, 2, 128, 4
COL_F = 4 * FOX_W
COL_Z = COL_F + FOX_H
COL_X = COL_Z + SSD_W
COL_B = COL_X + SSD_W
COL_C = COL_B + SSD_G * SSD_N
COL_DT = COL_C + SSD_G * SSD_N
SSD_FIRST = [c + g * SSD_N for g in range(SSD_G) for c in (COL_B, COL_C)]
HG_W, HG_H = 2048, 16
FOX_COLS = [2 * FOX_W, FOX_W, 0, 3 * FOX_W]
HG_COLS = [2 * HG_W, HG_W, 0, 3 * HG_W]
LEVELS = [1, 2, 4, 8, 16, 32, 64]
DT_ROW = 32
GATE_ROWS = 64
FAR = -1e30


def until(e, sem, value):
    if isinstance(value, int):
        if value > 0:
            e.wait_ge(sem, value)
        return
    e.wait_ge(sem, value)
    e.sem_inc(e.passed, 1)


class Steps:

    def __init__(self, e, sem):
        self.e, self.sem, self.n = e, sem, 0

    def do(self, ins):
        ins.then_inc(self.sem, 1)
        self.n += 1
        return self.n

    def after(self, n=None):
        n = self.n if n is None else n
        if n:
            self.e.wait_ge(self.sem, n)

    def restart(self):
        if self.n:
            self.e.wait_ge(self.sem, self.n)
            self.e.sem_clear(self.sem)
        self.n = 0


def turns(e, count, body):
    body(0, False)
    with e.Fori(1, count - 1) as i:
        body(i, False)
    body(count - 1, True)


def cols(start, size):
    return bass.ds(start, size)


def tiles(ap, n=NT):
    return ap.rearrange("p (n c) -> p n c", n=n)


class Core:

    def __init__(self, nc, ctx):
        self.nc, self.ctx = nc, ctx
        sb = self.sb
        self.uT = sb("uT", [P, 2, KT, T], F32R)
        self.ident = sb("ident", [P, P])
        self.ones = sb("ones", [P, P])
        self.tri = sb("tri", [P, P])
        self.last = sb("last", [P, P])
        self.dt, self.acum, self.out_dec, self.state_dec, self.chunk_dec = (
            sb(n, [P, NT, SSD_H]) for n in ("dt", "acum", "out_dec", "state_dec", "chunk_dec"))
        self.proj = [self.pb(f"proj{i}") for i in range(2)]
        self.ps = self.pb("ps", T)
        self.pt = self.pb("pt", T)
        self.pm = self.pb("pm", T)
        self.y_dram = nc.dram_tensor("mixed", (YT, P, T), F32, kind="Internal").ap()
        self.h_dram = nc.dram_tensor("hidden", (T, D), F32, kind="Internal").ap()
        self.fox_rows = nc.dram_tensor("fox_rows", (FOX_H, T), F32, kind="Internal").ap()
        self.ssd_rows = nc.dram_tensor("ssd_rows", (SSD_H, T), F32, kind="Internal").ap()

    def sb(self, name, shape, dtype=F32, ctx=None):
        return (ctx or self.ctx).enter_context(self.nc.sbuf_tensor(name, shape, dtype))

    def pb(self, name, n=HALF):
        return self.ctx.enter_context(self.nc.psum_tensor(name, [P, n], F32))


class Phase:

    def __init__(self, core, name, slab=None):
        self.core, self.name, self.ctx = core, name, ExitStack()
        self.used = list(slab.used) if slab else []

    def __enter__(self):
        self.ctx.__enter__()
        return self

    def __exit__(self, *a):
        nc = self.core.nc
        self.block.__exit__(*a)
        nc.clear_and_free_semaphores(self.used)
        nc.all_engine_barrier()
        return self.ctx.__exit__(*a)

    def open_block(self):
        self.block = self.core.nc.Block()
        return self.block.__enter__()

    def sb(self, name, shape, dtype=F32):
        return self.core.sb(f"{self.name}_{name}", shape, dtype, self.ctx)

    def sems(self, names):
        made = [self.core.nc.alloc_semaphore(name=f"{self.name}_{n}") for n in names.split()]
        self.used += made
        return made

    def own(self):
        return self.sems("dve_steps pool_steps act_passed dve_passed pool_passed pe_passed sp_passed")


class Slabs:

    def __init__(self, core, ctx, name, w, first):
        self.core, self.w, self.first = core, w, first
        tile = lambda n, dtype: [core.sb(f"{name}_{n}{b}", [P, KT, P], dtype, ctx) for b in range(2)]
        self.raw, self.hi, self.lo = tile("raw", F32), tile("hi", F32R), tile("lo", F32R)
        self.used = [core.nc.alloc_semaphore(name=f"{name}_{n}") for n in (
            "raw0_loaded", "raw1_loaded", "hi_ready", "lo_ready", "half0_done", "half1_done")]
        l0, l1, self.hi_ready, self.lo_ready, p0, p1 = self.used
        self.loaded, self.done = [l0, l1], [p0, p1]

    def begin_loads(self, e):
        for n in range(2):
            self.load(e, n, n, self.first[n])

    def begin_hi(self, e):
        self.split_hi(e, 0, 0)

    def begin_lo(self, e):
        self.split_lo(e, 0, 0)

    def begin_portion(self, e, part):
        self.portion(e, 0, 0, 0, None, part)

    def load(self, e, n, b, col):
        until(e, self.lo_ready, n - 1)
        e.dma_start(self.raw[b][:, :, :], self.w[:, :, cols(col, P)]).then_inc(self.loaded[b], 16)

    def split_hi(self, e, n, b, turn=None):
        until(e, self.loaded[b], ((n // 2 if turn is None else turn) + 1) * 16)
        until(e, self.done[1], n - 1)
        e.activation(self.hi[b][:, :, :], self.raw[b][:, :, :], ACT.Copy).then_inc(self.hi_ready, 1)

    def split_lo(self, e, n, b):
        until(e, self.hi_ready, n + 1)
        e.tensor_tensor(self.lo[b][:, :, :], self.raw[b][:, :, :], self.hi[b][:, :, :].bitcast(F32),
                        ALU.subtract).then_inc(self.lo_ready, 1)

    def portion(self, e, n, b, half, free=None, part=None):
        u, out = self.core.uT, self.core.proj[half][:, :]
        first, end = (0, KT) if part is None else (part * KT // 2, (part + 1) * KT // 2)
        if first == 0:
            if half == 0:
                until(e, self.lo_ready, n + 1)
            if free:
                until(e, *free)
        t = slice(half * HALF, (half + 1) * HALF)
        for k in range(first, end):
            e.matmul(out, self.hi[b][:, k, :], u[:, 0, k, t], start=(k == 0), stop=False)
            e.matmul(out, self.hi[b][:, k, :], u[:, 1, k, t], start=False, stop=False)
            mm = e.matmul(out, self.lo[b][:, k, :], u[:, 0, k, t], start=False, stop=(k == KT - 1))
        if end == KT:
            mm.then_inc(self.done[half], 1)


def constants(core):
    with Phase(core, "const") as ph:
        nc = core.nc
        made, = ph.sems("made")
        block = ph.open_block()

        @block.gpsimd
        def _(pool):
            for tile, value in ((core.ident, 0.0), (core.ones, 1.0), (core.tri, 1.0), (core.last, 0.0)):
                pool.memset(tile[:, :], value).then_inc(made, 1)
            pool.wait_ge(made, 4)
            pool.affine_select(out=core.ident[:, :], in_=core.ident[:, :], compare_op=ALU.not_equal, fill=1.0,
                               base=0, pattern=[[-1, P]], channel_multiplier=1).then_inc(made, 1)
            pool.affine_select(out=core.tri[:, :], in_=core.tri[:, :], compare_op=ALU.is_ge, fill=0.0,
                               base=0, pattern=[[1, P]], channel_multiplier=-1).then_inc(made, 1)
            pool.affine_select(out=core.last[:, :], in_=core.last[:, :], compare_op=ALU.not_equal, fill=1.0,
                               base=-(P - 1), pattern=[[0, P]], channel_multiplier=1).then_inc(made, 1)
            pool.wait_ge(made, 7)


def norm_phase(core, name, h_dram, w_row, upcoming):
    with Phase(core, name) as ph:
        nc, uT = core.nc, core.uT
        w_all, power = ph.sb("w_all", [P, D]), ph.sb("power", [P, 1])
        h = [ph.sb(f"h{b}", [P, D]) for b in range(4)]
        xn, junk = ([ph.sb(f"{n}{b}", [P, D]) for b in range(3)] for n in ("xn", "junk"))
        sumsq, mean, rstd = (ph.sb(n, [P, NT]) for n in ("sumsq", "mean", "rstd"))
        banks = [core.ps, core.pm, core.pt]
        w_loaded, sq_ready, mean_ready, rstd_ready, xn_ready, turned, hi_ready, lo_ready, power_set = ph.sems(
            "w_loaded sq_ready mean_ready rstd_ready xn_ready turned hi_ready lo_ready power_set")
        h_loaded = ph.sems("h0_loaded h1_loaded h2_loaded h3_loaded")
        block = ph.open_block()

        @block.sync
        def _(sp):
            for i in range(NT):
                until(sp, xn_ready, i - 3)
                sp.dma_start(h[i % 4][:, :], h_dram[i * P:(i + 1) * P, :]).then_inc(h_loaded[i % 4], 16)
                if i == 0:
                    sp.dma_start(w_all[:, :], w_row.partition_broadcast(P)).then_inc(w_loaded, 16)

        @block.scalar
        def _(act):
            def square(i):
                act.wait_ge(h_loaded[i % 4], (i // 4 + 1) * 16)
                until(act, sq_ready, i - 2)
                act.activation(junk[i % 3][:, :], h[i % 4][:, :], ACT.Square,
                               accum_out=sumsq[:, i:i + 1]).then_inc(sq_ready, 1)
            for i in range(3):
                square(i)
            upcoming.begin_loads(act)
            for i in range(NT):
                if i + 3 < NT:
                    square(i + 3)
                act.wait_ge(turned, i + 1)
                act.activation(uT[:, 0, :, i * P:(i + 1) * P], tiles(banks[i % 3][:, :]), ACT.Copy).then_inc(hi_ready, 1)
                if i == 2:
                    upcoming.begin_hi(act)

        @block.gpsimd
        def _(pool):
            pool.memset(power[:, :], -0.5).then_inc(power_set, 1)
            pool.wait_ge(power_set, 1)
            for i in range(NT):
                pool.wait_ge(sq_ready, i + 1)
                pool.tensor_scalar(mean[:, i:i + 1], sumsq[:, i:i + 1], 1.0 / D, EPS, ALU.mult,
                                   ALU.add).then_inc(mean_ready, 1)
                pool.wait_ge(mean_ready, i + 1)
                pool.tensor_tensor(rstd[:, i:i + 1], mean[:, i:i + 1], power[:, :], ALU.pow).then_inc(rstd_ready, 1)
                if i == 5:
                    upcoming.begin_lo(pool)

        @block.vector
        def _(dve):
            def scale(i):
                dve.wait_ge(rstd_ready, i + 1)
                until(dve, turned, i - 2)
                dve.scalar_tensor_tensor(out=xn[i % 3][:, :], in0=h[i % 4][:, :], scalar=rstd[:, i:i + 1],
                                         in1=w_all[:, :], op0=ALU.mult, op1=ALU.mult).then_inc(xn_ready, 1)
            dve.wait_ge(w_loaded, 16)
            scale(0)
            scale(1)
            for i in range(NT):
                if i + 2 < NT:
                    scale(i + 2)
                t = slice(i * P, (i + 1) * P)
                dve.wait_ge(hi_ready, i + 1)
                dve.tensor_tensor(uT[:, 1, :, t], tiles(banks[i % 3][:, :]), uT[:, 0, :, t].bitcast(F32),
                                  ALU.subtract).then_inc(lo_ready, 1)

        @block.tensor
        def _(pe):
            for i in range(NT):
                pe.wait_ge(xn_ready, i + 1)
                until(pe, lo_ready, i - 2)
                for k in range(KT):
                    mm = pe.transpose(banks[i % 3][:, k * P:(k + 1) * P], xn[i % 3][:, k * P:(k + 1) * P],
                                      core.ident[:, :])
                mm.then_inc(turned, 1)
                if i >= NT - 2:
                    pe.wait_ge(lo_ready, NT // 2)
                    upcoming.begin_portion(pe, i - (NT - 2))


def rows_of(w):
    return w.rearrange("(k p) n -> p k n", p=P)


class Gates:

    def __init__(self, ph, even_w_in, fox_f_bias, ssd_dt_bias, ssd_A_log):
        self.core, self.w = ph.core, rows_of(even_w_in)
        self.fox_f_bias, self.ssd_dt_bias, self.ssd_A_log = fox_f_bias, ssd_dt_bias, ssd_A_log
        self.raw = ph.sb("narrow_raw", [P, KT, GATE_ROWS])
        self.hi, self.lo = (ph.sb(f"narrow_{n}", [P, KT, GATE_ROWS], F32R) for n in ("hi", "lo"))
        self.x, self.mag, self.soft, self.run, self.keep = (
            ph.sb(n, [GATE_ROWS, T]) for n in ("x", "mag", "soft", "run", "keep"))
        self.bias, self.a_col = ph.sb("bias", [GATE_ROWS, 1]), ph.sb("a_col", [GATE_ROWS, 1])
        (self.zeroed, self.small, self.hi_made, self.lo_made, self.done0, self.done1, self.x_ready, self.mag_ready,
         self.log_ready, self.run_ready, self.stored, self.turned, self.a_ready, self.nat_ready, self.spread,
         self.diff_ready, self.decays, self.dt_scaled) = ph.sems(
            "zeroed small hi_made lo_made rows0_done rows1_done x_ready mag_ready log_ready run_ready stored "
            "turned a_ready nat_ready spread diff_ready decays dt_scaled")
        self.chunk_end = self.core.pt[:, 0:NT * SSD_H].rearrange("p (c h) -> p c h", c=NT)
        self.dt, self.fox = slice(DT_ROW, DT_ROW + SSD_H), slice(0, FOX_H)

    def zero(self, pool):
        for tile in (self.raw[:, :, :], self.bias[:, :], self.a_col[:, :]):
            pool.memset(tile, 0.0).then_inc(self.zeroed, 1)

    def load(self, sp):
        sp.wait_ge(self.zeroed, 3)
        with self.core.nc.allow_non_contiguous_dma(reason="a few short columns"):
            for tile, source in (
                    (self.raw[:, :, self.fox], self.w[:, :, COL_F:COL_F + FOX_H]),
                    (self.raw[:, :, self.dt], self.w[:, :, COL_DT:COL_DT + SSD_H]),
                    (self.bias[self.fox, :], self.fox_f_bias.rearrange("(h a) -> h a", a=1)),
                    (self.bias[self.dt, :], self.ssd_dt_bias.rearrange("(h a) -> h a", a=1)),
                    (self.a_col[self.dt, :], self.ssd_A_log.rearrange("(h a) -> h a", a=1))):
                sp.dma_start(tile, source).then_inc(self.small, 16)

    def store(self, sp):
        sp.wait_ge(self.run_ready, 2)
        sp.dma_start(self.core.fox_rows, self.run[self.fox, :]).then_inc(self.stored, 16)
        sp.dma_start(self.core.ssd_rows, self.run[self.dt, :]).then_inc(self.stored, 16)
        sp.wait_ge(self.stored, 32)

    def split_hi(self, act):
        act.wait_ge(self.small, 16 * 5)
        act.activation(self.hi[:, :, :], self.raw[:, :, :], ACT.Copy).then_inc(self.hi_made, 1)

    def split_lo(self, dve):
        dve.wait_ge(self.hi_made, 1)
        dve.tensor_tensor(self.lo[:, :, :], self.raw[:, :, :], self.hi[:, :, :].bitcast(F32),
                          ALU.subtract).then_inc(self.lo_made, 1)

    def products(self, pe, free):
        pe.wait_ge(self.lo_made, 1)
        u = self.core.uT
        for half in range(2):
            t, out = slice(half * HALF, (half + 1) * HALF), self.core.proj[half][0:GATE_ROWS, :]
            pe.wait_ge(free, half + 1)
            for k in range(KT):
                pe.matmul(out, self.hi[:, k, :], u[:, 0, k, t], start=(k == 0), stop=False)
                pe.matmul(out, self.hi[:, k, :], u[:, 1, k, t], start=False, stop=False)
                mm = pe.matmul(out, self.lo[:, k, :], u[:, 0, k, t], start=False, stop=(k == KT - 1))
            mm.then_inc((self.done0, self.done1)[half], 1)

    def evacuate(self, act):
        act.activation(self.a_col[:, :], self.a_col[:, :], ACT.Exp).then_inc(self.a_ready, 1)
        for half in range(2):
            act.wait_ge((self.done0, self.done1)[half], 1)
            act.activation(self.x[:, half * HALF:(half + 1) * HALF], self.core.proj[half][0:GATE_ROWS, :],
                           ACT.Identity, bias=self.bias[:, :]).then_inc(self.x_ready, 1)

    def log(self, act):
        act.wait_ge(self.mag_ready, 1)
        act.activation(self.mag[:, :], self.mag[:, :], ACT.Exp, scale=-1.0).then_inc(self.log_ready, 1)
        act.wait_ge(self.log_ready, 1)
        act.activation(self.mag[:, :], self.mag[:, :], ACT.Ln, bias=1.0).then_inc(self.log_ready, 1)

    def sums(self, dve, step):
        x, dt, fox = self.x, self.dt, self.fox
        step.do(dve.memset(self.keep[:, :], 1.0))
        step.do(dve.memset(self.run[:, :], 0.0))
        step.after()
        step.do(dve.memset(self.keep[dt, 0:T:P], 0.0))
        dve.wait_ge(self.x_ready, 2)
        step.do(dve.tensor_scalar(x[fox, :], x[fox, :], -1.0, None, ALU.mult))
        step.after()
        dve.scalar_tensor_tensor(out=self.mag[:, :], in0=x[:, :], scalar=-1.0, in1=x[:, :], op0=ALU.mult,
                                 op1=ALU.max).then_inc(self.mag_ready, 1)
        dve.wait_ge(self.log_ready, 2)
        step.do(dve.scalar_tensor_tensor(out=self.soft[:, :], in0=x[:, :], scalar=0.0, in1=self.mag[:, :],
                                         op0=ALU.max, op1=ALU.add))
        dve.wait_ge(self.a_ready, 1)
        step.after()
        step.do(dve.tensor_scalar(x[dt, :], self.soft[dt, :], self.a_col[dt, :], -1.0, ALU.mult, ALU.mult))
        dve.tensor_tensor_scan(self.run[fox, :], self.keep[fox, :], self.soft[fox, :], 0.0, ALU.mult,
                               ALU.add).then_inc(self.run_ready, 1)
        step.after()
        dve.tensor_tensor_scan(self.run[dt, :], self.keep[dt, :], x[dt, :], 0.0, ALU.mult,
                               ALU.add).then_inc(self.run_ready, 1)

    def turn(self, pe):
        pe.wait_ge(self.run_ready, 2)
        for n, src in enumerate((self.soft, self.run)):
            for c in range(NT):
                at = n * HALF + c * GATE_ROWS
                mm = pe.transpose(self.core.ps[:, at:at + GATE_ROWS], src[:, c * P:(c + 1) * P],
                                  self.core.ident[0:GATE_ROWS, 0:GATE_ROWS])
        mm.then_inc(self.turned, 1)

    def keep_natural(self, dve):
        dve.wait_ge(self.turned, 1)
        view = self.core.ps[:, :].rearrange("p (a c r) -> p a c r", a=2, c=NT)
        dve.tensor_copy(self.core.dt[:, :, :], view[:, 0, :, self.dt]).then_inc(self.nat_ready, 1)
        dve.tensor_copy(self.core.acum[:, :, :], view[:, 1, :, self.dt]).then_inc(self.nat_ready, 1)

    def ends(self, pe):
        pe.wait_ge(self.nat_ready, 2)
        pe.matmul(self.core.pt[:, 0:NT * SSD_H], self.core.last[:, :],
                  self.core.acum[:, :, :].rearrange("p c h -> p (c h)"), start=True, stop=True).then_inc(self.spread, 1)

    def subtract(self, dve):
        dve.wait_ge(self.nat_ready, 2)
        dve.wait_ge(self.spread, 1)
        dve.tensor_tensor(self.core.state_dec[:, :, :], self.chunk_end, self.core.acum[:, :, :],
                          ALU.subtract).then_inc(self.diff_ready, 1)

    def exps(self, act):
        act.wait_ge(self.nat_ready, 2)
        act.activation(self.core.out_dec[:, :, :], self.core.acum[:, :, :], ACT.Exp).then_inc(self.decays, 1)
        act.wait_ge(self.diff_ready, 1)
        act.activation(self.core.chunk_dec[:, :, :], self.chunk_end, ACT.Exp).then_inc(self.decays, 1)
        act.activation(self.core.state_dec[:, :, :], self.core.state_dec[:, :, :], ACT.Exp).then_inc(self.decays, 1)

    def scale(self, dve):
        dve.wait_ge(self.decays, 3)
        dve.tensor_tensor(self.core.state_dec[:, :, :], self.core.state_dec[:, :, :], self.core.dt[:, :, :],
                          ALU.mult).then_inc(self.dt_scaled, 1)
        dve.wait_ge(self.dt_scaled, 1)

    def banks_free(self, pe):
        pe.wait_ge(self.nat_ready, 2)
        pe.wait_ge(self.decays, 3)


def fox_phase(core, slab, upcoming, even_w_in, fox_f_bias, ssd_dt_bias, ssd_A_log):
    with Phase(core, "fox", slab) as ph:
        nc = core.nc
        gates = Gates(ph, even_w_in, fox_f_bias, ssd_dt_bias, ssd_A_log)
        ps, pt, pm = core.ps, core.pt, core.pm
        qT, k_new, kT, gT, vT, v, logit, prob, probT, o_nat, yT, sig, bias_all, bias_diag = (
            ph.sb(n, [P, T]) for n in
            "qT k_new kT gT vT v logit prob probT o_nat yT sig bias_all bias_diag".split())
        far = ph.sb("far", [P, P])
        row_max, neg_max, row_sum, inv_sum = (ph.sb(n, [P, NT]) for n in ("row_max", "neg_max", "row_sum", "inv_sum"))
        off_max = ph.sb("off_max", [P, NT])
        (vT_ready, v_turned, v_ready, k_new_ready, k_ready, q_ready, scores_done, logits_ready, probs_ready,
         probs_turned, probT_ready, pv_done, o_scaled, o_turned, y_ready, y_stored, bias_loaded, g_ready,
         sig_ready, far_set) = ph.sems(
            "vT_ready v_turned v_ready k_new_ready k_ready q_ready scores_done logits_ready probs_ready "
            "probs_turned probT_ready pv_done o_scaled o_turned y_ready y_stored bias_loaded g_ready "
            "sig_ready far_set")
        dve_steps, pool_steps, act_passed, dve_passed, pool_passed, pe_passed, sp_passed = ph.own()
        COLS, S = FOX_COLS, len(FOX_COLS)
        free = [None, vT_ready, k_new_ready, q_ready]

        def at_step(i, q):
            return (i, 2 * (S - 1) + q) if q < 2 else (i + 1, q - 2)
        block = ph.open_block()

        @block.sync
        def _(sp):
            sp.passed = sp_passed
            gates.load(sp)
            gates.store(sp)
            sp.dma_start(bias_all[:, :], core.fox_rows[0, :].partition_broadcast(P)).then_inc(bias_loaded, 16)

            def head(i, last):
                if not last:
                    until(sp, logits_ready, (i + 1) * NT)
                    row = core.fox_rows[cols(i + 1, 1), :].rearrange("a t -> (a t)")
                    sp.dma_start(bias_all[:, :], row.partition_broadcast(P)).then_inc(bias_loaded, 16)
                until(sp, y_ready, (i + 1) * 2)
                sp.dma_start(core.y_dram[cols(i, 1), :, :].rearrange("a p t -> p (a t)"), yT[:, :]).then_inc(y_stored, 16)
            turns(sp, FOX_H, head)
            sp.wait_ge(y_stored, 16 * FOX_H)

        @block.gpsimd
        def _(pool):
            pool.passed = pool_passed
            gates.zero(pool)
            pool.memset(far[:, :], 0.0).then_inc(far_set, 1)
            pool.wait_ge(far_set, 1)
            pool.affine_select(out=far[:, :], in_=far[:, :], compare_op=ALU.is_ge, fill=FAR, base=0,
                               pattern=[[-1, P]], channel_multiplier=1).then_inc(far_set, 1)

            def copy_k(i):
                until(pool, k_new_ready, (i + 1) * 2)
                pool.tensor_copy(kT[:, :], k_new[:, :]).then_inc(k_ready, 1)

            for j in range(1, S):
                slab.split_lo(pool, j, j % 2)
            copy_k(0)

            def head(i, last):
                if not last:
                    for j in range(S):
                        slab.split_lo(pool, (i + 1) * S + j, j % 2)
                    until(pool, scores_done, (i + 1) * NT)
                    copy_k(i + 1)
            turns(pool, FOX_H, head)
            upcoming.begin_lo(pool)

        @block.scalar
        def _(act):
            act.passed = act_passed

            def ahead(i, j, what):
                n = i * S + j
                if what == 0:
                    slab.split_hi(act, n + 1, (j + 1) % 2, i * (S // 2) + (j + 1) // 2)
                else:
                    h2 = (i + (j + 2) // S) % FOX_H
                    slab.load(act, n + 2, j % 2, h2 * P + COLS[(j + 2) % S])

            def evacuate(i, p):
                j, half = p // 2, p % 2
                t, bank = slice(half * HALF, (half + 1) * HALF), core.proj[half][:, :]
                until(act, slab.done[half], i * S + j + 1)
                if j == 0:
                    until(act, v_turned, i)
                    act.activation(vT[:, t], bank, ACT.Copy).then_inc(vT_ready, 1)
                elif j == 1:
                    until(act, k_ready, i)
                    act.activation(k_new[:, t], bank, ACT.Copy).then_inc(k_new_ready, 1)
                elif j == 2:
                    act.activation(qT[:, t], bank, ACT.Copy, scale=FOX_D ** -0.5).then_inc(q_ready, 1)
                else:
                    until(act, g_ready, i * 2)
                    act.activation(sig[:, t], bank, ACT.Sigmoid).then_inc(sig_ready, 1)

            upcoming.begin_loads(act)
            gates.split_hi(act)
            for j in range(S - 1):
                ahead(0, j, 0)
                ahead(0, j, 1)
                evacuate(0, 2 * j)
                evacuate(0, 2 * j + 1)
                if j == 0:
                    gates.evacuate(act)
                    gates.log(act)
            gates.exps(act)

            def copy_probT(i, q):
                w = (q + 1) * P
                until(act, probs_turned, i * NT + q + 1)
                until(act, pv_done, i * NT + q)
                act.activation(probT[:, 0:w], pt[:, 0:w], ACT.Copy).then_inc(probT_ready, 1)

            def head(i, last):
                until(act, v_turned, i + 1)
                act.activation(v[:, :], pt[:, :], ACT.Copy).then_inc(v_ready, 1)
                for q in range(NT):
                    if not last:
                        ahead(*((i, S - 1) if q < 2 else (i + 1, q // 2 - 1)), q % 2)
                    if 1 <= q <= 2 or q and not last:
                        evacuate(*at_step(i, q - 1))
                    if q:
                        copy_probT(i, q - 1)
                    w = (q + 1) * P
                    until(act, logits_ready, i * NT + q + 1)
                    until(act, probs_turned, i * NT + q)
                    act.activation(prob[:, 0:w], logit[:, 0:w], ACT.Exp, bias=neg_max[:, q:q + 1],
                                   accum_out=row_sum[:, q:q + 1]).then_inc(probs_ready, 1)
                copy_probT(i, NT - 1)
                if not last:
                    evacuate(*at_step(i, NT - 1))
            turns(act, FOX_H, head)
            upcoming.begin_hi(act)
            act.wait_ge(slab.loaded[0], 16 * (FOX_H * S // 2 + 1))

        @block.vector
        def _(dve):
            dve.passed = dve_passed
            step = Steps(dve, dve_steps)
            gates.split_lo(dve)
            gates.sums(dve, step)

            def gate(i, half):
                until(dve, sig_ready, i * 2 + half + 1)
                until(dve, y_ready, i * 2)
                t = slice(half * HALF, (half + 1) * HALF)
                dve.tensor_tensor(gT[:, t], core.proj[half][:, :], sig[:, t], ALU.mult).then_inc(g_ready, 1)

            gates.keep_natural(dve)
            gates.subtract(dve)
            gates.scale(dve)
            dve.wait_ge(far_set, 2)
            step.restart()

            def scale(i, q):
                until(dve, pv_done, i * NT + q + 1)
                step.do(dve.reciprocal(inv_sum[:, q:q + 1], row_sum[:, q:q + 1]))
                step.after()
                dve.tensor_scalar(o_nat[:, q * P:(q + 1) * P], pm[:, (q % 2) * HALF:(q % 2) * HALF + P],
                                  inv_sum[:, q:q + 1], None, ALU.mult).then_inc(o_scaled, 1)

            def head(i, last):
                until(dve, bias_loaded, (i + 1) * 16)
                step.do(dve.tensor_tensor(tiles(bias_diag[:, :]), tiles(bias_all[:, :]),
                                          far[:, :].unsqueeze(1).to_broadcast([P, NT, P]), ALU.add))
                for q in range(NT):
                    w, d = q * P, slice(q * P, (q + 1) * P)
                    until(dve, scores_done, i * NT + q + 1)
                    until(dve, probs_ready, i * NT + q)
                    if q:
                        step.do(dve.tensor_tensor_reduce(logit[:, 0:w], ps[:, 0:w], bias_all[:, 0:w], 1.0, FAR, ALU.add,
                                                         ALU.max, off_max[:, q:q + 1]))
                    step.after()
                    first = off_max[:, q:q + 1] if q else FAR
                    step.do(dve.tensor_tensor_reduce(logit[:, d], ps[:, d], bias_diag[:, d], 1.0, first, ALU.add,
                                                     ALU.max, row_max[:, q:q + 1]))
                    step.after()
                    dve.tensor_scalar(neg_max[:, q:q + 1], row_max[:, q:q + 1], -1.0, None,
                                      ALU.mult).then_inc(logits_ready, 1)
                    if q in (1, 2):
                        gate(i, q - 1)
                    if q >= 2:
                        scale(i, q - 2)
                scale(i, NT - 2)
                scale(i, NT - 1)
                until(dve, o_turned, i + 1)
                until(dve, g_ready, (i + 1) * 2)
                until(dve, y_stored, i * 16)
                for half in range(2):
                    t = slice(half * HALF, (half + 1) * HALF)
                    dve.tensor_tensor(yT[:, t], pm[:, t], gT[:, t], ALU.mult).then_inc(y_ready, 1)
                step.restart()
            turns(dve, FOX_H, head)

        @block.tensor
        def _(pe):
            pe.passed = pe_passed

            def portion(i, p, part=None):
                j, half = p // 2, p % 2
                read = (g_ready, (i - 1) * 2 + half + 1) if j == 0 else (free[j], i * 2 + half + 1)
                if isinstance(i, int) and i == 0 and j < 2:
                    read = (gates.x_ready, half + 1) if j else None
                slab.portion(pe, i * S + j, j % 2, half, read, part)

            for p in range(1, 2 * (S - 1)):
                portion(0, p)
                if p == 1:
                    gates.products(pe, vT_ready)
                if p == 4:
                    gates.turn(pe)
                if p == 5:
                    gates.ends(pe)
            gates.banks_free(pe)

            def turn_probs(i, q):
                until(pe, probs_ready, i * NT + q + 1)
                until(pe, probT_ready, i * NT + q)
                if q == 0:
                    until(pe, v_ready, i + 1)
                for s in range(q + 1):
                    mm = pe.transpose(pt[:, s * P:(s + 1) * P], prob[:, s * P:(s + 1) * P], core.ident[:, :])
                mm.then_inc(probs_turned, 1)

            def times_v(i, q):
                until(pe, probT_ready, i * NT + q + 1)
                if q >= 2:
                    until(pe, o_scaled, i * NT + q - 1)
                else:
                    until(pe, y_ready, i * 2)
                out = pm[:, (q % 2) * HALF:(q % 2) * HALF + P]
                for s in range(q + 1):
                    mm = pe.matmul(out, probT[:, s * P:(s + 1) * P], v[:, s * P:(s + 1) * P],
                                   start=(s == 0), stop=(s == q))
                mm.then_inc(pv_done, 1)

            def head(i, last):
                until(pe, vT_ready, (i + 1) * 2)
                until(pe, probT_ready, i * NT)
                for c in range(NT):
                    mm = pe.transpose(pt[:, c * P:(c + 1) * P], vT[:, c * P:(c + 1) * P], core.ident[:, :])
                mm.then_inc(v_turned, 1)
                for q in range(NT):
                    w = (q + 1) * P
                    if q == 0:
                        until(pe, k_ready, i + 1)
                    if q % 4 == 0:
                        until(pe, q_ready, i * 2 + q // 4 + 1)
                    until(pe, logits_ready, i * NT + q)
                    for s in range(0, w, HALF):
                        end = min(s + HALF, w)
                        mm = pe.matmul(ps[:, s:end], qT[:, q * P:(q + 1) * P], kT[:, s:end], start=True, stop=True)
                    mm.then_inc(scores_done, 1)
                    if q:
                        turn_probs(i, q - 1)
                    if q < 2 or not last:
                        portion(*at_step(i, q), None if q < NT - 1 else 0)
                    if q:
                        times_v(i, q - 1)
                turn_probs(i, NT - 1)
                if not last:
                    portion(*at_step(i, NT - 1), 1)
                times_v(i, NT - 1)
                until(pe, o_scaled, (i + 1) * NT)
                for c in range(NT):
                    mm = pe.transpose(pm[:, c * P:(c + 1) * P], o_nat[:, c * P:(c + 1) * P], core.ident[:, :])
                mm.then_inc(o_turned, 1)
            turns(pe, FOX_H, head)


def ssd_phase(core, slab, conv_w, conv_b, d_skip, ssd_norm_w):
    with Phase(core, "ssd", slab) as ph:
        nc = core.nc
        ps, pt, pm = core.ps, core.pt, core.pm
        PAIRS, GROUP, TAIL = SSD_H // 2, SSD_H // 2 // SSD_G, SSD_TAPS - 1
        x_in = ph.sb("x_in", [P, TAIL + T])
        (conv, sig, bT, x_new, xT, x_nat, xd, xdd, state, z_new, zT, zsig, sumsq, sqr) = (
            ph.sb(n, [P, T]) for n in
            "conv sig bT x_new xT x_nat xd xdd state z_new zT zsig sumsq sqr".split())
        cT, b_nat, cb = ([ph.sb(f"{n}{g}", [P, T]) for g in range(SSD_G)] for n in ("cT", "b_nat", "cb"))
        y_nat, rms = xdd, sqr
        decay = [ph.sb(f"decay{h}", [P, T]) for h in range(2)]
        y_all = ph.sb("y_all", [P, GROUP, T])
        SLABS = PAIRS + 2 * SSD_G
        taps, cbias = ph.sb("taps", [P, SLABS, SSD_TAPS]), ph.sb("cbias", [P, SLABS])
        skip, nw, eps = ph.sb("skip", [P, PAIRS]), ph.sb("nw", [P, PAIRS]), ph.sb("eps", [P, 1])
        (small, zeroed, acum_loaded, xin_ready, conv_ready, sig_ready, bc_ready, x_new_ready, xT_ready, x_turned,
         x_nat_ready, xdd_ready, sub_ready, diff_ready, exp_ready, decay_ready, b_turned, b_nat_ready, cb_done,
         cb_ready, sums_done, state_ready, y_done, y_nat_ready, y_turned, y_ready, zsig_ready, z_new_ready, z_ready,
         sqr_ready, sumsq_ready, total_done, rms_ready, out_ready, y_stored) = ph.sems(
            "small zeroed acum_loaded xin_ready conv_ready sig_ready bc_ready x_new_ready xT_ready x_turned "
            "x_nat_ready xdd_ready sub_ready diff_ready exp_ready decay_ready b_turned b_nat_ready cb_done "
            "cb_ready sums_done state_ready y_done y_nat_ready y_turned y_ready zsig_ready z_new_ready z_ready "
            "sqr_ready sumsq_ready total_done rms_ready out_ready y_stored")
        dve_steps, pool_steps, act_passed, dve_passed, pool_passed, pe_passed, sp_passed = ph.own()
        LEAD = 2 * SSD_G
        SMALL = 16 * (SSD_TAPS + 1 + 1 + 2)
        by_head = lambda ap: ap.rearrange("p (c h d) -> p c h d", c=NT, h=2)

        def pair_of(tile, i):
            return tile[:, :, cols(i * 2, 2)].unsqueeze(3).to_broadcast([P, NT, 2, SSD_P])

        def pairs(e, body):
            for g in range(SSD_G):
                body(g * GROUP, g, g > 0, False)
                with e.Fori(g * GROUP + 1, (g + 1) * GROUP - 1) as i:
                    body(i, g, False, False)
                body((g + 1) * GROUP - 1, g, False, g == SSD_G - 1)
        block = ph.open_block()

        @block.sync
        def _(sp):
            sp.passed = sp_passed
            with nc.allow_non_contiguous_dma(reason="per-channel parameters, a few kilobytes"):
                for k in range(SSD_TAPS):
                    sp.dma_start(taps[:, :, k], conv_w[k, :].rearrange("(s p) -> p s", p=P)).then_inc(small, 16)
                sp.dma_start(cbias[:, :], conv_b.rearrange("(s p) -> p s", p=P)).then_inc(small, 16)
                sp.dma_start(nw[:, :], ssd_norm_w.rearrange("(s p) -> p s", p=P)).then_inc(small, 16)
                for h in range(2):
                    sp.dma_start(skip[h * SSD_P:(h + 1) * SSD_P, :],
                                 d_skip[h:SSD_H:2].partition_broadcast(SSD_P)).then_inc(small, 16)

            def load_acum(i):
                for h in range(2):
                    row = core.ssd_rows[cols(i * 2 + h, 1), :].rearrange("a t -> (a t)")
                    sp.dma_start(decay[h][:, :], row.partition_broadcast(P)).then_inc(acum_loaded, 16)

            def store(g):
                for s in range(GROUP):
                    sp.wait_ge(out_ready, g * GROUP + s + 1)
                    sp.dma_start(core.y_dram[FOX_H + g * GROUP + s, :, :], y_all[:, s, :]).then_inc(y_stored, 16)
            load_acum(0)

            def pair(i, g, new_group, last):
                if new_group:
                    store(g - 1)
                if not last:
                    until(sp, y_done, i + 1)
                    load_acum(i + 1)
            pairs(sp, pair)
            store(SSD_G - 1)
            sp.wait_ge(y_stored, 16 * PAIRS)

        @block.gpsimd
        def _(pool):
            pool.passed = pool_passed
            pool.memset(x_in[:, 0:TAIL], 0.0).then_inc(zeroed, 1)
            pool.memset(eps[:, :], EPS).then_inc(zeroed, 1)
            pool.sem_inc(sumsq_ready, 1)

            def subtract(i):
                until(pool, acum_loaded, (i + 1) * 32)
                for h in range(2):
                    a = core.acum[:, :, cols(i * 2 + h, 1)].to_broadcast([P, NT, P])
                    pool.tensor_tensor(tiles(decay[h][:, :]), tiles(decay[h][:, :]), a, ALU.subtract
                                       ).then_inc(sub_ready, 1)
            for n in range(1, LEAD):
                slab.split_lo(pool, n, n % 2)
            subtract(0)
            for n in range(LEAD, LEAD + 3):
                slab.split_lo(pool, n, n % 2)

            def pair(i, g, new_group, last):
                if not last:
                    for j in range(2):
                        slab.split_lo(pool, i * 2 + (LEAD + 3 + j), (1 + j) % 2)
                if not last:
                    subtract(i + 1)
                until(pool, sqr_ready, i + 1)
                if isinstance(i, int) and i % GROUP == 0:
                    if g:
                        pool.wait_ge(total_done, g)
                    pool.tensor_copy(sumsq[:, :], sqr[:, :]).then_inc(sumsq_ready, 1)
                else:
                    until(pool, sumsq_ready, i + 1)
                    pool.tensor_tensor(sumsq[:, :], sumsq[:, :], sqr[:, :], ALU.add).then_inc(sumsq_ready, 1)
            pairs(pool, pair)

        @block.scalar
        def _(act):
            act.passed = act_passed
            act.wait_ge(zeroed, 2)

            def evac_conv(m, n, half):
                until(act, slab.done[half], n + 1)
                until(act, conv_ready, m)
                act.activation(x_in[:, TAIL + half * HALF:TAIL + (half + 1) * HALF], core.proj[half][:, :],
                               ACT.Copy).then_inc(xin_ready, 1)

            def sigmoid(m):
                until(act, conv_ready, m + 1)
                act.activation(sig[:, :], conv[:, :], ACT.Sigmoid).then_inc(sig_ready, 1)

            def evac_z(i, n, half):
                t = slice(half * HALF, (half + 1) * HALF)
                until(act, slab.done[half], n + 1)
                until(act, z_new_ready, i * 2)
                act.activation(zsig[:, t], core.proj[half][:, :], ACT.Sigmoid).then_inc(zsig_ready, 1)

            def b_out(g):
                act.wait_ge(b_turned, g + 1)
                act.activation(b_nat[g][:, :], pt[:, :], ACT.Copy).then_inc(b_nat_ready, 1)

            first = SSD_FIRST + [COL_X, COL_Z, COL_X + P, COL_Z + P]
            for n in range(LEAD + 2):
                slab.split_hi(act, n + 1, (n + 1) % 2)
                slab.load(act, n + 2, n % 2, first[n + 2])
                for half in range(2):
                    if n < LEAD + 1:
                        evac_conv(n, n, half)
                    else:
                        evac_z(0, n, half)
                if n < LEAD + 1:
                    sigmoid(n)
                if n == LEAD - 2:
                    b_out(0)
                if n == LEAD:
                    b_out(1)

            def root(g):
                act.wait_ge(total_done, g + 1)
                act.activation(rms[:, :], ps[:, :], ACT.Sqrt, scale=1.0 / (GROUP * P),
                               bias=eps[:, :]).then_inc(rms_ready, 1)

            def squares(i, at, g):
                until(act, y_ready, i + 1)
                until(act, sumsq_ready, i + 1)
                if g:
                    act.wait_ge(out_ready, g * GROUP)
                act.activation(sqr[:, :], y_all[:, cols(at, 1), :].rearrange("p a t -> p (a t)"),
                               ACT.Square).then_inc(sqr_ready, 1)

            def pair(i, g, new_group, last):
                until(act, x_turned, i + 1)
                until(act, y_ready, i)
                act.activation(x_nat[:, :], pt[:, :], ACT.Copy).then_inc(x_nat_ready, 1)
                if new_group:
                    squares(i - 1, GROUP - 1, g - 1)
                elif not (isinstance(i, int) and i == 0):
                    squares(i - 1, i - (g * GROUP + 1), g)
                act.activation(xT[:, :], x_new[:, :], ACT.Copy).then_inc(xT_ready, 1)
                until(act, z_new_ready, (i + 1) * 2)
                act.activation(zT[:, :], z_new[:, :], ACT.Copy).then_inc(z_ready, 1)
                for h in range(2):
                    until(act, diff_ready, i * 2 + h + 1)
                    act.activation(decay[h][:, :], decay[h][:, :], ACT.Exp).then_inc(exp_ready, 1)
                if new_group:
                    root(g - 1)
                if not last:
                    i2 = (i + 2) % PAIRS
                    n = i * 2 + (LEAD + 2)
                    slab.split_hi(act, n + 1, 1, i + (LEAD // 2 + 1))
                    slab.load(act, n + 2, 0, i2 * P + COL_X)
                    evac_conv(i + (LEAD + 1), n, 0)
                    evac_conv(i + (LEAD + 1), n, 1)
                    sigmoid(i + (LEAD + 1))
                    slab.split_hi(act, n + 2, 0, i + (LEAD // 2 + 2))
                    slab.load(act, n + 3, 1, i2 * P + COL_Z)
                    evac_z(i + 1, n + 1, 0)
                    evac_z(i + 1, n + 1, 1)
            pairs(act, pair)
            squares(PAIRS - 1, GROUP - 1, SSD_G - 1)
            root(SSD_G - 1)
            for b in range(2):
                act.wait_ge(slab.loaded[b], 16 * (PAIRS + LEAD // 2 + 1))

        @block.vector
        def _(dve):
            dve.passed = dve_passed
            step = Steps(dve, dve_steps)
            dve.wait_ge(small, SMALL)

            def convolve(m, at, used, count):
                until(dve, xin_ready, (m + 1) * 2)
                until(dve, used, count)
                w = lambda k: taps[:, cols(at, 1), k]
                step.do(dve.tensor_scalar(conv[:, :], x_in[:, TAIL:TAIL + T], w(TAIL), cbias[:, cols(at, 1)],
                                          ALU.mult, ALU.add))
                for k in range(TAIL):
                    step.after()
                    ins = dve.scalar_tensor_tensor(out=conv[:, :], in0=x_in[:, k:k + T], scalar=w(k),
                                                   in1=conv[:, :], op0=ALU.mult, op1=ALU.add)
                    if k < TAIL - 1:
                        step.do(ins)
                ins.then_inc(conv_ready, 1)

            def silu(m, out, ready):
                until(dve, sig_ready, m + 1)
                dve.tensor_tensor(out[:, :], conv[:, :], sig[:, :], ALU.mult).then_inc(ready, 1)

            def gate(i, half):
                t = slice(half * HALF, (half + 1) * HALF)
                until(dve, zsig_ready, i * 2 + half + 1)
                until(dve, z_ready, i)
                dve.tensor_tensor(z_new[:, t], core.proj[half][:, :], zsig[:, t], ALU.mult).then_inc(z_new_ready, 1)

            def mask(g):
                dve.wait_ge(cb_done, g + 1)
                dve.tensor_tensor(tiles(cb[g][:, :]), tiles(ps[:, :]), core.tri[:, :].unsqueeze(1).to_broadcast([P, NT, P]),
                                  ALU.mult).then_inc(cb_ready, 1)

            for g in range(SSD_G):
                convolve(2 * g, PAIRS + g, bc_ready, 2 * g)
                if g:
                    dve.wait_ge(cb_done, g)
                silu(2 * g, bT, bc_ready)
                if g:
                    mask(g - 1)
                convolve(2 * g + 1, PAIRS + SSD_G + g, bc_ready, 2 * g + 1)
                silu(2 * g + 1, cT[g], bc_ready)
            convolve(LEAD, 0, bc_ready, LEAD)
            silu(LEAD, x_new, x_new_ready)
            mask(SSD_G - 1)
            gate(0, 0)
            gate(0, 1)
            dve.wait_ge(cb_ready, SSD_G)
            step.restart()

            def clip(i, h):
                until(dve, sub_ready, i * 2 + h + 1)
                dve.tensor_scalar(decay[h][:, :], decay[h][:, :], 0.0, None, ALU.min).then_inc(diff_ready, 1)

            def finish(g):
                dve.wait_ge(rms_ready, g + 1)
                step.do(dve.reciprocal(rms[:, :], rms[:, :]))
                step.after()
                for s in range(GROUP):
                    at = g * GROUP + s
                    dve.scalar_tensor_tensor(out=y_all[:, s, :], in0=y_all[:, s, :], scalar=nw[:, at:at + 1],
                                             in1=rms[:, :], op0=ALU.mult, op1=ALU.mult).then_inc(out_ready, 1)

            def pair(i, g, new_group, last):
                until(dve, x_nat_ready, i + 1)
                dve.tensor_tensor(by_head(xdd[:, :]), by_head(x_nat[:, :]), pair_of(core.state_dec, i),
                                  ALU.mult).then_inc(xdd_ready, 1)
                clip(i, 0)
                clip(i, 1)
                step.do(dve.tensor_tensor(by_head(xd[:, :]), by_head(x_nat[:, :]), pair_of(core.dt, i), ALU.mult))
                for h in range(2):
                    until(dve, exp_ready, i * 2 + h + 1)
                    dve.tensor_tensor(decay[h][:, :], decay[h][:, :], cb[g][:, :], ALU.mult).then_inc(decay_ready, 1)
                until(dve, sums_done, i + 1)
                step.do(dve.tensor_copy(state[:, P:2 * P], pm[:, 0:P]))
                for c in range(1, NT - 1):
                    step.after()
                    for h in range(2):
                        now, nxt = c * P + h * SSD_P, (c + 1) * P + h * SSD_P
                        ins = dve.scalar_tensor_tensor(
                            out=state[:, nxt:nxt + SSD_P], in0=state[:, now:now + SSD_P],
                            scalar=core.chunk_dec[:, c, cols(i * 2 + h, 1)],
                            in1=pm[:, now:now + SSD_P], op0=ALU.mult, op1=ALU.add)
                        if c < NT - 2 or h == 0:
                            step.do(ins)
                ins.then_inc(state_ready, 1)
                if new_group:
                    finish(g - 1)
                if not last:
                    until(dve, xT_ready, i + 1)
                    convolve(i + (LEAD + 1), i + 1, x_new_ready, i + 1)
                until(dve, y_done, i + 1)
                rest = lambda ap: by_head(ap)[:, 1:NT, :, :]
                step.do(dve.tensor_tensor(rest(y_nat[:, :]), rest(ps[:, :]), pair_of(core.out_dec, i)[:, 1:NT, :, :],
                                          ALU.mult))
                step.do(dve.tensor_copy(y_nat[:, 0:P], pt[:, 0:P]))
                step.after()
                dve.tensor_tensor(y_nat[:, P:T], y_nat[:, P:T], pt[:, P:T], ALU.add).then_inc(y_nat_ready, 1)
                if not last:
                    silu(i + (LEAD + 1), x_new, x_new_ready)
                    gate(i + 1, 0)
                until(dve, y_turned, i + 1)
                step.do(dve.scalar_tensor_tensor(out=x_nat[:, :], in0=xT[:, :], scalar=skip[:, cols(i, 1)],
                                                 in1=pm[:, :], op0=ALU.mult, op1=ALU.add))
                until(dve, z_ready, i + 1)
                if new_group:
                    dve.wait_ge(y_stored, 16 * g * GROUP)
                step.after()
                dve.tensor_tensor(y_all[:, cols(i - g * GROUP, 1), :].rearrange("p a t -> p (a t)"), x_nat[:, :],
                                  zT[:, :], ALU.mult).then_inc(y_ready, 1)
                if not last:
                    gate(i + 1, 1)
                step.restart()
            pairs(dve, pair)
            finish(SSD_G - 1)

        @block.tensor
        def _(pe):
            pe.passed = pe_passed

            def turn(bank, src, ready):
                for c in range(NT):
                    mm = pe.transpose(bank[:, c * P:(c + 1) * P], src[:, c * P:(c + 1) * P], core.ident[:, :])
                mm.then_inc(ready, 1)

            def lead(n):
                for half in range(2):
                    slab.portion(pe, n, n % 2, half, (xin_ready, (n - 1) * 2 + half + 1) if n else None)

            def group_products(g):
                pe.wait_ge(bc_ready, 2 * g + 1)
                if g:
                    pe.wait_ge(b_nat_ready, g)
                turn(pt, bT, b_turned)
                pe.wait_ge(bc_ready, 2 * g + 2)
                if g:
                    pe.wait_ge(cb_ready, g)
                for c in range(NT):
                    t = slice(c * P, (c + 1) * P)
                    mm = pe.matmul(ps[:, t], bT[:, t], cT[g][:, t], start=True, stop=True)
                mm.then_inc(cb_done, 1)

            lead(0)
            lead(1)
            lead(2)
            group_products(0)
            lead(3)
            lead(4)
            group_products(1)
            lead(5)

            def total(g):
                pe.wait_ge(sumsq_ready, (g + 1) * GROUP + 1)
                for half in range(2):
                    t = slice(half * HALF, (half + 1) * HALF)
                    mm = pe.matmul(ps[:, t], core.ones[:, :], sumsq[:, t], start=True, stop=True)
                mm.then_inc(total_done, 1)

            def pair(i, g, new_group, last):
                def portion(j, half):
                    if not last:
                        free = (z_new_ready, i * 2 + half + 1) if j == 0 else (xin_ready, (i + (LEAD + 1)) * 2 + half + 1)
                        slab.portion(pe, i * 2 + (LEAD + 2 + j), j, half, free)

                until(pe, x_new_ready, i + 1)
                if isinstance(i, int) and i == 0:
                    pe.wait_ge(b_nat_ready, SSD_G)
                until(pe, y_nat_ready, i)
                turn(pt, x_new, x_turned)
                portion(0, 0)
                until(pe, y_ready, i)
                until(pe, xdd_ready, i + 1)
                for c in range(NT - 1):
                    t = slice(c * P, (c + 1) * P)
                    mm = pe.matmul(pm[:, t], b_nat[g][:, t], xdd[:, t], start=True, stop=True)
                mm.then_inc(sums_done, 1)
                if new_group:
                    total(g - 1)
                portion(0, 1)
                until(pe, decay_ready, (i + 1) * 2)
                until(pe, state_ready, i + 1)
                if isinstance(i, int) and i == 0:
                    pe.wait_ge(cb_ready, SSD_G)
                if new_group:
                    pe.wait_ge(rms_ready, g)
                for c in range(NT):
                    t = slice(c * P, (c + 1) * P)
                    if c:
                        pe.matmul(ps[:, t], cT[g][:, t], state[:, t], start=True, stop=True)
                    for h in range(2):
                        th = slice(c * P + h * SSD_P, c * P + (h + 1) * SSD_P)
                        mm = pe.matmul(pt[:, th], decay[h][:, t], xd[:, th], start=True, stop=True)
                mm.then_inc(y_done, 1)
                portion(1, 0)
                until(pe, y_nat_ready, i + 1)
                turn(pm, y_nat, y_turned)
                portion(1, 1)
            pairs(pe, pair)
            total(SSD_G - 1)


def out_phase(core, name, w_out, h_dram, final_w, dst):
    with Phase(core, name) as ph:
        nc = core.nc
        final = final_w is not None
        SWEEPS, J, GROUP = 2, NT // 2, 4
        GROUPS = YT // GROUP
        w_hi = ph.sb("w_hi", [P, YT, D], F32R)
        w_lo = core.uT[:, :, :, :].rearrange("p a k t -> p (a k) t")
        y_raw = [ph.sb(f"y_raw{b}", [P, HALF]) for b in range(2)]
        y_hi, y_lo = (ph.sb(n, [P, 2 * GROUP, HALF], F32R) for n in ("y_hi", "y_lo"))
        w_raw = [ph.sb(f"w_raw{b}", [P, D]) for b in range(2)]
        h = [ph.sb(f"h{j}", [P, D]) for j in range(J)]
        w_all, junk = (ph.sb(n, [P, D]) for n in ("w_all", "junk")) if final else (None, None)
        sumsq, mean, rstd = (ph.sb(n, [P, J]) for n in ("sumsq", "mean", "rstd"))
        power = ph.sb("power", [P, 1])
        banks = [[bank[:, 0:HALF], bank[:, HALF:T]] for bank in (core.ps, core.pt, core.pm)]
        banks.append([core.proj[0][:, :], core.proj[1][:, :]])
        (small, w_hi_ready, w_lo_ready, y_hi_ready, y_lo_ready, group_done, tile_done, h_ready, sq_ready,
         rstd_ready, out_ready, power_set) = ph.sems(
            "small w_hi_ready w_lo_ready y_hi_ready y_lo_ready group_done tile_done h_ready sq_ready "
            "rstd_ready out_ready power_set")
        w_loaded, y_loaded = ph.sems("w0_loaded w1_loaded"), ph.sems("y0_loaded y1_loaded")
        h_loaded, stored = ph.sems("h0_loaded h1_loaded h2_loaded h3_loaded"), ph.sems("stored0 stored1 stored2 stored3")
        dve_steps, pool_steps, act_passed, dve_passed, pool_passed, pe_passed, sp_passed = ph.own()
        block = ph.open_block()

        @block.sync
        def _(sp):
            for s in range(SWEEPS):
                for k in range(YT):
                    n = s * YT + k
                    until(sp, y_lo_ready, n - 1)
                    sp.dma_start(y_raw[n % 2][:, :], core.y_dram[k, :, s * HALF:(s + 1) * HALF]
                                 ).then_inc(y_loaded[n % 2], 16)
                    if k in range(GROUP, GROUP + J):
                        j = k - GROUP
                        until(sp, stored[j], 16 * s)
                        row = (s * J + j) * P
                        sp.dma_start(h[j][:, :], h_dram[row:row + P, :]).then_inc(h_loaded[j], 16)
                if s == 0 and final:
                    sp.dma_start(w_all[:, :], final_w.partition_broadcast(P)).then_inc(small, 16)

        @block.gpsimd
        def _(pool):
            for k in range(YT):
                until(pool, w_lo_ready, k - 1)
                pool.dma_start(w_raw[k % 2][:, :], w_out[k * P:(k + 1) * P, :]).then_inc(w_loaded[k % 2], 16)
            pool.memset(power[:, :], -0.5).then_inc(power_set, 1)
            pool.wait_ge(power_set, 1)
            step = Steps(pool, pool_steps)
            for s in range(SWEEPS):
                for j in range(J):
                    n = s * J + j + 1
                    if final:
                        pool.wait_ge(sq_ready, n)
                        step.do(pool.tensor_scalar(mean[:, j:j + 1], sumsq[:, j:j + 1], 1.0 / D, EPS, ALU.mult, ALU.add))
                        step.after()
                        pool.tensor_tensor(rstd[:, j:j + 1], mean[:, j:j + 1], power[:, :], ALU.pow).then_inc(rstd_ready, 1)
                    pool.wait_ge(*((out_ready, n) if final else (h_ready, 2 * (J + n))))
                    row = (s * J + j) * P
                    pool.dma_start(dst[row:row + P, :], h[j][:, :]).then_inc(stored[j], 16)
            for j in range(J):
                pool.wait_ge(stored[j], 16 * SWEEPS)

        @block.scalar
        def _(act):
            def split_y(s, k):
                n = s * YT + k
                act.wait_ge(y_loaded[n % 2], (n // 2 + 1) * 16)
                until(act, group_done, n // GROUP - 1)
                act.activation(y_hi[:, n % (2 * GROUP), :], y_raw[n % 2][:, :], ACT.Copy).then_inc(y_hi_ready, 1)

            for k in range(YT):
                split_y(0, k)
                act.wait_ge(w_loaded[k % 2], (k // 2 + 1) * 16)
                act.activation(w_hi[:, k, :], w_raw[k % 2][:, :], ACT.Copy).then_inc(w_hi_ready, 1)

            def squares(s):
                for j in range(J):
                    act.wait_ge(h_ready, 2 * ((s + 1) * J + j + 1))
                    if s * J + j:
                        act.wait_ge(sq_ready, s * J + j)
                    act.activation(junk[:, :], h[j][:, :], ACT.Square,
                                   accum_out=sumsq[:, j:j + 1]).then_inc(sq_ready, 1)
            for k in range(YT):
                split_y(1, k)
                if final and k == GROUP - 1:
                    squares(0)
            if final:
                squares(1)

        @block.vector
        def _(dve):
            def split_y(s, k):
                n = s * YT + k
                dve.wait_ge(y_hi_ready, n + 1)
                slot = n % (2 * GROUP)
                dve.tensor_tensor(y_lo[:, slot, :], y_raw[n % 2][:, :], y_hi[:, slot, :].bitcast(F32),
                                  ALU.subtract).then_inc(y_lo_ready, 1)

            def finish(s):
                def scale(j):
                    dve.wait_ge(rstd_ready, s * J + j + 1)
                    dve.scalar_tensor_tensor(out=h[j][:, :], in0=h[j][:, :], scalar=rstd[:, j:j + 1],
                                             in1=w_all[:, :], op0=ALU.mult, op1=ALU.mult).then_inc(out_ready, 1)
                for j in range(J):
                    dve.wait_ge(tile_done, s * J + j + 1)
                    dve.wait_ge(h_loaded[j], 16 * (s + 1))
                    for half in range(2):
                        t = slice(half * HALF, (half + 1) * HALF)
                        dve.tensor_tensor(h[j][:, t], banks[j][half], h[j][:, t], ALU.add).then_inc(h_ready, 1)
                    if final and j:
                        scale(j - 1)
                if final:
                    scale(J - 1)

            dve.sem_inc(h_ready, 2 * J)
            for k in range(YT):
                split_y(0, k)
                dve.wait_ge(w_hi_ready, k + 1)
                dve.tensor_tensor(w_lo[:, k, :], w_raw[k % 2][:, :], w_hi[:, k, :].bitcast(F32),
                                  ALU.subtract).then_inc(w_lo_ready, 1)
            if final:
                dve.wait_ge(small, 16)
            for k in range(YT):
                split_y(1, k)
                if k == GROUP - 1:
                    finish(0)
            finish(1)

        @block.tensor
        def _(pe):
            pe.passed = pe_passed

            def products(j, k):
                slot, t = k % (2 * GROUP), slice(j * P, (j + 1) * P)
                parts = (y_hi, w_hi[:, k]), (y_hi, w_lo[:, k]), (y_lo, w_hi[:, k])
                for n, (y, w) in enumerate(parts):
                    for half in range(2):
                        mm = pe.matmul(banks[j][half], y[:, slot, t], w[:, half * HALF:(half + 1) * HALF],
                                       start=(k == 0 and n == 0), stop=(k == YT - 1 and n == 2))
                return mm

            def sweep(s):
                for g in range(GROUPS):
                    ks = range(g * GROUP, (g + 1) * GROUP)
                    order = [(j, k) for k in ks for j in range(J)] if g == 0 else [(j, k) for j in range(J) for k in ks]
                    for j, k in order:
                        if j == 0:
                            pe.wait_ge(w_lo_ready, k + 1)
                            until(pe, y_lo_ready, s * YT + (k + 1))
                        if k == 0:
                            until(pe, h_ready, s * (2 * J) + (j + 1) * 2)
                        mm = products(j, k)
                        if k == YT - 1:
                            mm.then_inc(tile_done, 1)
                        elif j == J - 1 and k == ks[-1]:
                            mm.then_inc(group_done, 1)
                    if g == GROUPS - 1:
                        until(pe, tile_done, s * J + J)
                        pe.sem_inc(group_done, 1)
            with pe.Fori(0, SWEEPS) as s:
                sweep(s)


def hgrn_phase(core, slab, lb_logits, norm_w):
    with Phase(core, "hgrn", slab) as ph:
        nc = core.nc
        ps, pt, pm = core.ps, core.pt, core.pm
        qT, kT, fT, halves_prod, scores, vT, v, k_nat, state, o_nat, sig, sqr, gT, yT = (
            ph.sb(n, [P, T]) for n in
            "qT kT fT halves_prod scores vT v k_nat state o_nat sig sqr gT yT".split())
        q2 = ph.sb("q2", [P, NT, P])
        first_mask = ph.sb("first_mask", [P, P], mybir.dt.int8)
        masks = ph.sb("masks", [P, len(LEVELS), P // 2], mybir.dt.int8)
        lb, rest, lb_tmp, lb_inv = (ph.sb(n, [P, HG_H]) for n in ("lb", "rest", "lb_tmp", "lb_inv"))
        nw, power = ph.sb("nw", [P, 1]), ph.sb("power", [P, NT])
        sumsq, mean, rstd = (ph.sb(n, [P, NT]) for n in ("sumsq", "mean", "rstd"))
        (small, made, lb_diff, lb_exp, vT_ready, v_turned, v_ready, sig_ready, g_ready, f_raw_ready,
         f_ready, q_ready, level_done, level_ready, scores_ready, k_turned, k_nat_ready, sums_done, state_ready,
         o_done, sq_ready, sumsq_ready, rstd_ready, o_nat_ready, o_turned, y_ready, y_stored, qsig_ready) = ph.sems(
            "small made lb_diff lb_exp vT_ready v_turned v_ready sig_ready g_ready f_raw_ready "
            "f_ready q_ready level_done level_ready scores_ready k_turned k_nat_ready sums_done state_ready "
            "o_done sq_ready sumsq_ready rstd_ready o_nat_ready o_turned y_ready y_stored qsig_ready")
        dve_steps, pool_steps, act_passed, dve_passed, pool_passed, pe_passed, sp_passed = ph.own()
        COLS, S = HG_COLS, len(HG_COLS)
        L = len(LEVELS)
        prod = {1: fT[:, :]}
        at = 0
        for h in LEVELS:
            prod[2 * h] = halves_prod[:, at:at + T // (2 * h)]
            at += T // (2 * h)
        block = ph.open_block()

        def side(ap, h, right):
            return ap.rearrange("p (b two h) -> p b two h", two=2, h=h)[:, :, int(right), :]

        def rights(ap, h):
            return ap.rearrange("p (c b two h) -> p c b two h", c=NT, two=2, h=h)[:, :, :, 1, :]

        def every(mask, h):
            return mask.rearrange("p (b h) -> p b h", h=h).unsqueeze(1).to_broadcast([P, NT, P // (2 * h), h])

        def parity(ap, odd, n=NT):
            return ap.rearrange("p (c j two) -> p c j two", c=n, two=2)[:, :, :, int(odd)]

        @block.sync
        def _(sp):
            sp.passed = sp_passed
            with nc.allow_non_contiguous_dma(reason="per-channel parameters, a few kilobytes"):
                sp.dma_start(lb[:, :], lb_logits[0, :].rearrange("(h k) -> k h", k=P)).then_inc(small, 16)
                sp.dma_start(nw[:, :], norm_w.rearrange("(v a) -> v a", a=1)).then_inc(small, 16)
            with sp.Fori(0, HG_H) as i:
                until(sp, y_ready, (i + 1) * 2)
                sp.dma_start(core.y_dram[cols(i, 1), :, :].rearrange("a p t -> p (a t)"), yT[:, :]).then_inc(y_stored, 16)
            sp.wait_ge(y_stored, 16 * HG_H)

        @block.gpsimd
        def _(pool):
            pool.passed = pool_passed
            def lower(j):
                h = LEVELS[j]
                pool.affine_select(out=masks[:, j, :], in_=masks[:, j, :], compare_op=ALU.is_ge, fill=0.0, base=0,
                                   pattern=[[-2 * h, P // (2 * h)], [0, h]],
                                   channel_multiplier=1).then_inc(made, 1)

            def upper(j):
                h = LEVELS[j]
                pool.wait_ge(made, 7 + j)
                pool.affine_select(out=masks[:, j, :], in_=masks[:, j, :], compare_op=ALU.is_ge, fill=0.0, base=h - 1,
                                   pattern=[[2 * h, P // (2 * h)], [0, h]],
                                   channel_multiplier=-1).then_inc(made, 1)

            pool.memset(scores[:, :], 0.0).then_inc(made, 1)
            pool.memset(power[:, :], -0.5).then_inc(made, 1)
            pool.memset(first_mask[:, :], 0.0).then_inc(made, 1)
            pool.memset(masks[:, 0, :], 0.0).then_inc(made, 1)
            pool.memset(masks[:, 1:, :], 1.0).then_inc(made, 1)
            slab.split_lo(pool, 1, 1)
            pool.wait_ge(made, 5)
            pool.affine_select(out=first_mask[:, :], in_=first_mask[:, :], compare_op=ALU.not_equal, fill=1.0, base=0,
                               pattern=[[-2, P // 2], [0, 2]], channel_multiplier=1).then_inc(made, 1)
            pool.affine_select(out=masks[:, 0, :], in_=masks[:, 0, :], compare_op=ALU.not_equal, fill=1.0, base=-1,
                               pattern=[[-2, P // 2]], channel_multiplier=1).then_inc(made, 1)
            slab.split_lo(pool, 2, 0)
            for j in range(1, len(LEVELS)):
                lower(j)
            for j in range(1, len(LEVELS)):
                upper(j)
            slab.split_lo(pool, 3, 1)
            step = Steps(pool, pool_steps)

            def head(i, last):
                if not last:
                    for j in range(3):
                        slab.split_lo(pool, (i + 1) * S + j, j % 2)
                until(pool, sumsq_ready, i + 1)
                step.do(pool.tensor_scalar(mean[:, :], sumsq[:, :], 1.0 / P, EPS, ALU.mult, ALU.add))
                step.after()
                pool.tensor_tensor(rstd[:, :], mean[:, :], power[:, :], ALU.pow).then_inc(rstd_ready, 1)
                if not last:
                    slab.split_lo(pool, (i + 1) * S + 3, 1)
                step.restart()
            turns(pool, HG_H, head)

        @block.scalar
        def _(act):
            act.passed = act_passed

            def ahead(i, j):
                n = i * S + j
                slab.split_hi(act, n + 1, (j + 1) % 2, i * (S // 2) + (j + 1) // 2)
                h2 = (i + (j + 2) // S) % HG_H
                slab.load(act, n + 2, j % 2, h2 * P + COLS[(j + 2) % S])

            def evacuate(i, p):
                j, half = p // 2, p % 2
                t, bank = slice(half * HALF, (half + 1) * HALF), core.proj[half][:, :]
                until(act, slab.done[half], i * S + j + 1)
                if j == 0:
                    until(act, v_turned, i)
                    act.activation(vT[:, t], bank, ACT.Copy).then_inc(vT_ready, 1)
                elif j == 1:
                    until(act, scores_ready, i)
                    act.activation(fT[:, t], bank, ACT.Sigmoid).then_inc(f_raw_ready, 1)
                    act.activation(kT[:, t], bank, ACT.Sigmoid, scale=-1.0).then_inc(f_raw_ready, 1)
                elif j == 2:
                    until(act, g_ready, i * 2)
                    act.activation(sig[:, t], bank, ACT.Sigmoid).then_inc(qsig_ready, 1)
                else:
                    until(act, q_ready, (i + 1) * 2)
                    act.activation(sig[:, t], bank, ACT.Sigmoid).then_inc(sig_ready, 1)

            for j in range(S - 1):
                ahead(0, j)
                if j == 0:
                    act.wait_ge(lb_diff, 1)
                    act.activation(lb_tmp[:, :], lb_tmp[:, :], ACT.Exp).then_inc(lb_exp, 1)
                evacuate(0, 2 * j)
                evacuate(0, 2 * j + 1)

            def head(i, last):
                until(act, v_turned, i + 1)
                act.activation(v[:, :], pt[:, :], ACT.Copy).then_inc(v_ready, 1)
                if not last:
                    ahead(i, 3)
                evacuate(i, 6)
                evacuate(i, 7)
                if not last:
                    ahead(i + 1, 0)
                    evacuate(i + 1, 0)
                    evacuate(i + 1, 1)
                until(act, k_turned, i + 1)
                act.activation(k_nat[:, :], pt[:, :], ACT.Copy).then_inc(k_nat_ready, 1)
                if not last:
                    ahead(i + 1, 1)
                    evacuate(i + 1, 2)
                    evacuate(i + 1, 3)
                until(act, o_done, i + 1)
                act.activation(sqr[:, :], ps[:, :], ACT.Square).then_inc(sq_ready, 1)
                if not last:
                    ahead(i + 1, 2)
                    evacuate(i + 1, 4)
                    evacuate(i + 1, 5)
            turns(act, HG_H, head)
            act.wait_ge(slab.loaded[0], 16 * (HG_H * S // 2 + 1))

        @block.vector
        def _(dve):
            dve.passed = dve_passed
            step = Steps(dve, dve_steps)
            dve.wait_ge(small, 32)
            dve.tensor_tensor(lb_tmp[:, :], lb[:, :], lb[:, :], ALU.subtract).then_inc(lb_diff, 1)
            dve.wait_ge(lb_exp, 1)
            step.do(dve.reciprocal(lb_inv[:, :], lb_tmp[:, :]))
            step.after()
            step.do(dve.tensor_tensor(lb_tmp[:, :], lb_tmp[:, :], lb_inv[:, :], ALU.mult))
            step.after()
            step.do(dve.tensor_tensor(lb[:, :], lb_tmp[:, :], lb_tmp[:, :], ALU.subtract))
            step.after()
            step.do(dve.tensor_scalar(rest[:, :], lb[:, :], -1.0, 1.0, ALU.mult, ALU.add))
            step.restart()

            def gate(i, half):
                t = slice(half * HALF, (half + 1) * HALF)
                until(dve, sig_ready, i * 2 + half + 1)
                until(dve, y_ready, i * 2)
                dve.tensor_tensor(gT[:, t], core.proj[half][:, :], sig[:, t], ALU.mult).then_inc(g_ready, 1)

            def bound(i, half):
                t = slice(half * HALF, (half + 1) * HALF)
                until(dve, f_raw_ready, i * 4 + half * 2 + 2)
                dve.tensor_scalar(fT[:, t], fT[:, t], rest[:, cols(i, 1)], lb[:, cols(i, 1)], ALU.mult,
                                  ALU.add).then_inc(f_ready, 1)
                dve.tensor_scalar(kT[:, t], kT[:, t], rest[:, cols(i, 1)], None, ALU.mult).then_inc(f_ready, 1)

            def silu_q(i, half):
                t = slice(half * HALF, (half + 1) * HALF)
                until(dve, qsig_ready, i * 2 + half + 1)
                bank, n = core.proj[half][:, :], NT // 2
                odd_q = q2[:, half * n:(half + 1) * n, 0:P // 2]
                step.do(dve.tensor_tensor(odd_q, parity(bank, True, n), parity(sig[:, t], True, n), ALU.mult))
                step.do(dve.tensor_tensor(parity(qT[:, t], False, n), parity(bank, False, n),
                                          parity(sig[:, t], False, n), ALU.mult))
                step.after(step.n - 1)
                dve.tensor_tensor(parity(qT[:, t], True, n), odd_q, parity(fT[:, t], True, n),
                                  ALU.mult).then_inc(q_ready, 1)

            for half in range(2):
                bound(0, half)
            for half in range(2):
                silu_q(0, half)
            dve.wait_ge(made, 5 + 2 * len(LEVELS))
            step.restart()

            def head(i, last):
                def widen(j):
                    h = LEVELS[j]
                    wide = [P, T // (2 * h), h]
                    left = prod[h][:, 0::2].unsqueeze(2).to_broadcast(wide)
                    right = prod[h][:, 1::2].unsqueeze(2).to_broadcast(wide)
                    step.do(dve.tensor_tensor(side(qT[:, :], h, True), side(qT[:, :], h, True), left, ALU.mult))
                    return dve.tensor_tensor(side(kT[:, :], h, False), side(kT[:, :], h, False), right, ALU.mult)

                def double(j):
                    h = LEVELS[j]
                    if 2 * h < P:
                        step.do(dve.tensor_tensor(prod[4 * h], prod[2 * h][:, 0::2], prod[2 * h][:, 1::2], ALU.mult))

                until(dve, f_ready, (i + 1) * 4)
                step.do(dve.tensor_tensor(prod[2], fT[:, 0:T:2], fT[:, 1:T:2], ALU.mult))
                until(dve, level_done, i * L + 1)
                even_q = parity(qT[:, :], False)
                step.do(dve.tensor_tensor(even_q, even_q, parity(fT[:, :], False), ALU.mult))
                step.do(widen(0))
                step.after()
                dve.tensor_copy(q2[:, :, P // 2:P].rearrange("p c (b h) -> p c b h", h=2),
                                rights(qT[:, :], 2)).then_inc(level_ready, 1)
                double(0)
                step.do(dve.copy_predicated(tiles(scores[:, :]), first_mask[:, :].unsqueeze(1).to_broadcast([P, NT, P]),
                                            tiles(ps[:, :])))
                until(dve, level_done, i * L + 2)
                step.after()
                widen(1).then_inc(level_ready, 1)
                double(1)
                both = pm[:, :].rearrange("p (c w) -> p c w", c=NT)
                step.do(dve.copy_predicated(parity(scores[:, :], True),
                                            masks[:, 0, :].unsqueeze(1).to_broadcast([P, NT, P // 2]), both[:, :, 0:P // 2]))
                step.after()
                step.do(dve.copy_predicated(rights(scores[:, :], 2), every(masks[:, 1, :], 2),
                                            both[:, :, P // 2:P].rearrange("p c (b h) -> p c b h", h=2)))
                gate(i, 0)
                for j, h in enumerate(LEVELS):
                    if j < 2:
                        continue
                    until(dve, level_done, i * L + j + 1)
                    step.after()
                    widen(j).then_inc(level_ready, 1)
                    double(j)
                    bank = ps[:, (j % 2) * HALF:(j % 2 + 1) * HALF].rearrange("p (c b h) -> p c b h", c=NT, h=h)
                    ins = dve.copy_predicated(rights(scores[:, :], h), every(masks[:, j, :], h), bank)
                    if h == LEVELS[-1]:
                        ins.then_inc(scores_ready, 1)
                    else:
                        step.do(ins)
                    if j == 2:
                        gate(i, 1)
                until(dve, sums_done, i + 1)
                step.do(dve.tensor_copy(state[:, P:2 * P], pm[:, 0:P]))
                for c in range(1, NT - 1):
                    step.after()
                    ins = dve.scalar_tensor_tensor(out=state[:, (c + 1) * P:(c + 2) * P], in0=state[:, c * P:(c + 1) * P],
                                                   scalar=prod[P][:, c:c + 1], in1=pm[:, c * P:(c + 1) * P],
                                                   op0=ALU.mult, op1=ALU.add)
                    if c < NT - 2:
                        step.do(ins)
                ins.then_inc(state_ready, 1)
                if not last:
                    bound(i + 1, 0)
                until(dve, sq_ready, i + 1)
                dve.tensor_reduce(sumsq[:, :], tiles(sqr[:, :]), AX.X, ALU.add).then_inc(sumsq_ready, 1)
                if not last:
                    bound(i + 1, 1)
                until(dve, rstd_ready, i + 1)
                dve.tensor_tensor(tiles(o_nat[:, :]), tiles(ps[:, :]), rstd[:, :].unsqueeze(2).to_broadcast([P, NT, P]),
                                  ALU.mult).then_inc(o_nat_ready, 1)
                until(dve, o_turned, i + 1)
                until(dve, g_ready, (i + 1) * 2)
                until(dve, y_stored, i * 16)
                for half in range(2):
                    t = slice(half * HALF, (half + 1) * HALF)
                    dve.scalar_tensor_tensor(out=yT[:, t], in0=pt[:, t], scalar=nw[:, :], in1=gT[:, t],
                                             op0=ALU.mult, op1=ALU.mult).then_inc(y_ready, 1)
                if not last:
                    silu_q(i + 1, 0)
                    silu_q(i + 1, 1)
                step.restart()
            turns(dve, HG_H, head)

        @block.tensor
        def _(pe):
            pe.passed = pe_passed

            def portion(i, p, part=None):
                j, half = p // 2, p % 2
                if j == 0:
                    free = None if isinstance(i, int) and i == 0 else (g_ready, (i - 1) * 2 + half + 1)
                else:
                    free = [(vT_ready, i * 2 + half + 1), (f_raw_ready, i * 4 + half * 2 + 2),
                            (q_ready, i * 2 + half + 1)][j - 1]
                slab.portion(pe, i * S + j, j % 2, half, free, part)

            for p in range(1, 2 * (S - 1)):
                portion(0, p)

            def turn(bank, src, ready):
                for c in range(NT):
                    mm = pe.transpose(bank[:, c * P:(c + 1) * P], src[:, c * P:(c + 1) * P], core.ident[:, :])
                mm.then_inc(ready, 1)

            def head(i, last):
                def next_part(n):
                    if n < 4:
                        portion(i, 2 * (S - 1) + n // 2, n % 2)
                    elif not last:
                        portion(i + 1, n // 2 - 2, n % 2)

                until(pe, vT_ready, (i + 1) * 2)
                until(pe, y_ready, i * 2)
                turn(pt, vT, v_turned)
                next_part(0)
                until(pe, q_ready, (i + 1) * 2)
                until(pe, f_ready, (i + 1) * 4)
                for c in range(NT):
                    t = slice(c * P, (c + 1) * P)
                    mm = pe.matmul(ps[:, t], kT[:, t], qT[:, t], start=True, stop=True)
                mm.then_inc(level_done, 1)
                next_part(1)
                next_part(2)
                until(pe, level_ready, i * L + 1)
                for c in range(NT):
                    t = slice(c * P, (c + 1) * P)
                    mm = pe.matmul(pm[:, t], kT[:, t], q2[:, c, :], start=True, stop=True)
                mm.then_inc(level_done, 1)
                next_part(3)
                for j, h in enumerate(LEVELS):
                    if j < 2:
                        continue
                    until(pe, level_ready, i * L + j)
                    for c in range(NT):
                        t = slice(c * P, (c + 1) * P)
                        out = ps[:, (j % 2) * HALF + c * (P // 2):(j % 2) * HALF + (c + 1) * (P // 2)]
                        mm = pe.matmul(out, kT[:, t], side(qT[:, t], h, True), start=True, stop=True)
                    mm.then_inc(level_done, 1)
                    next_part(j + 2)
                until(pe, level_ready, (i + 1) * L)
                until(pe, v_ready, i + 1)
                turn(pt, kT, k_turned)
                next_part(9)
                until(pe, k_nat_ready, i + 1)
                for c in range(NT - 1):
                    t = slice(c * P, (c + 1) * P)
                    mm = pe.matmul(pm[:, t], k_nat[:, t], v[:, t], start=True, stop=True)
                mm.then_inc(sums_done, 1)
                next_part(10)
                next_part(11)
                until(pe, state_ready, i + 1)
                until(pe, scores_ready, i + 1)
                for c in range(NT):
                    t = slice(c * P, (c + 1) * P)
                    mm = pe.matmul(ps[:, t], scores[:, t], v[:, t], start=True, stop=(c == 0))
                    if c:
                        mm = pe.matmul(ps[:, t], qT[:, t], state[:, t], start=False, stop=True)
                mm.then_inc(o_done, 1)
                for n in range(12, 14):
                    next_part(n)
                until(pe, o_nat_ready, i + 1)
                turn(pt, o_nat, o_turned)
                for n in range(14, 16):
                    next_part(n)
            turns(pe, HG_H, head)


_INS = ["x", "norm_w", "final_norm_w", "even_w_in", "even_w_out", "fox_f_bias", "ssd_conv_w", "ssd_conv_b",
        "ssd_dt_bias", "ssd_A_log", "ssd_D", "ssd_norm_w", "odd_w_in", "odd_w_out", "hgrn_lb_logits", "hgrn_norm_w"]


def trunk(nc, x, norm_w, final_norm_w, even_w_in, even_w_out, fox_f_bias, ssd_conv_w, ssd_conv_b,
          ssd_dt_bias, ssd_A_log, ssd_D, ssd_norm_w, odd_w_in, odd_w_out, hgrn_lb_logits, hgrn_norm_w, out):
    with ExitStack() as ctx:
        core = Core(nc, ctx)
        constants(core)
        with ExitStack() as for_ssd:
            ssd_slab = Slabs(core, for_ssd, "ssd_slab", rows_of(even_w_in[0]), SSD_FIRST)
            with ExitStack() as for_fox:
                fox_slab = Slabs(core, for_fox, "fox_slab", rows_of(even_w_in[0]), FOX_COLS)
                norm_phase(core, "norm0", x[0], norm_w[0], fox_slab)
                fox_phase(core, fox_slab, ssd_slab, even_w_in[0], fox_f_bias[0], ssd_dt_bias[0], ssd_A_log[0])
            ssd_phase(core, ssd_slab, ssd_conv_w[0], ssd_conv_b[0], ssd_D[0], ssd_norm_w[0])
        out_phase(core, "out0", even_w_out[0], x[0], None, core.h_dram)
        with ExitStack() as for_hgrn:
            hgrn_slab = Slabs(core, for_hgrn, "hgrn_slab", rows_of(odd_w_in[0]), HG_COLS)
            norm_phase(core, "norm1", core.h_dram, norm_w[1], hgrn_slab)
            hgrn_phase(core, hgrn_slab, hgrn_lb_logits, hgrn_norm_w[0])
        out_phase(core, "out1", odd_w_out[0], core.h_dram, final_norm_w, out[0])


def kernel(**inputs):
    import numpy as np
    import concourse.bacc as bacc
    from concourse.bass_utils import run_bass_kernel_spmd

    nc = bacc.Bacc("TRN2", target_bir_lowering=False, num_devices=1)
    arrays, args = {}, []
    for name in _INS:
        a = np.ascontiguousarray(inputs[name])
        arrays[f"in_{name}"] = a
        args.append(nc.dram_tensor(f"in_{name}", a.shape, mybir.dt.from_np(a.dtype), kind="ExternalInput").ap())
    args.append(nc.dram_tensor("out", (1, T, D), F32, kind="ExternalOutput").ap())
    trunk(nc, *args)
    result = run_bass_kernel_spmd(nc, [arrays], core_ids=[0])
    return result.results[0]["out"]
```
